# Optimizing a Trainium2 kernel written in Bass

```python
import math
import jax, jax.numpy as jnp
from jax import lax
import numpy as np

D_MODEL = 1024
BATCH = 1
SEQ = 512
DEPTH = 2

HEAD_DIM = 128
RET_HEADS = 4
MOBA_HEADS = 4
FOX_HEADS = 8
RET_WIDTH = RET_HEADS * HEAD_DIM
MOBA_WIDTH = MOBA_HEADS * HEAD_DIM
FOX_WIDTH = FOX_HEADS * HEAD_DIM
RET_CHUNK = 128
MOBA_BLOCK = 256
MOBA_TOPK = 3
MOBA_Q_CHUNK = 32
FOX_Q_BLOCK = 128
N_REL_BUCKETS = 32
REL_MAX_DISTANCE = 128
ROPE_BASE = 10000.0
RMS_EPS = 1e-6
GN_EPS = 1e-5
NEG = -1e30
FFN_HIDDEN = ((8 * D_MODEL + 3 * 256 - 1) // (3 * 256)) * 256
N_EVEN = (DEPTH + 1) // 2
N_ODD = DEPTH // 2
EVEN_IN = 4 * RET_WIDTH + 3 * MOBA_WIDTH
ODD_IN = 3 * FOX_WIDTH + FOX_HEADS

kernel_name = "hybrid_retention_moba_fox_block"

def rms_norm(x, g):
    xf = x.astype(jnp.float32)
    y = xf * lax.rsqrt(jnp.mean(xf * xf, axis=-1, keepdims=True) + RMS_EPS)
    return (y * g.astype(jnp.float32)).astype(x.dtype)

def split_heads(t, n_heads):
    b, s, _ = t.shape
    return t.reshape(b, s, n_heads, HEAD_DIM).transpose(0, 2, 1, 3).astype(jnp.float32)

def merge_heads(t):
    b, h, s, d = t.shape
    return t.transpose(0, 2, 1, 3).reshape(b, s, h * d)

def rotary(t, pos):
    d = t.shape[-1]
    inv_freq = jnp.power(ROPE_BASE, -jnp.arange(0, d, 2, dtype=jnp.float32) / d)
    ang = pos.astype(jnp.float32)[:, None] * inv_freq[None, :]
    cos, sin = jnp.cos(ang), jnp.sin(ang)
    t1, t2 = t[..., : d // 2], t[..., d // 2:]
    return jnp.concatenate([t1 * cos - t2 * sin, t1 * sin + t2 * cos], axis=-1)

def t5_bucket(rel):
    n = jnp.maximum(rel, 0)
    max_exact = N_REL_BUCKETS // 2
    nf = jnp.maximum(n, 1).astype(jnp.float32)
    large = max_exact + (jnp.log(nf / max_exact) / math.log(REL_MAX_DISTANCE / max_exact)
                         * (N_REL_BUCKETS - max_exact)).astype(jnp.int32)
    large = jnp.minimum(large, N_REL_BUCKETS - 1)
    return jnp.where(n < max_exact, n, large)

def retention(q, k, v, pos):
    b, h, s, d = q.shape
    c = RET_CHUNK
    n = s // c
    log_g = jnp.log1p(-jnp.power(2.0, -5.0 - jnp.arange(h, dtype=jnp.float32)))
    q = rotary(q, pos) * (d ** -0.5)
    k = rotary(k, pos)
    idx = jnp.arange(c, dtype=jnp.float32)
    diff = idx[:, None] - idx[None, :]
    inner = jnp.where(diff >= 0, jnp.exp(log_g[:, None, None] * jnp.maximum(diff, 0.0)), 0.0)
    q_dec = jnp.exp(log_g[:, None] * (idx + 1.0))[:, :, None]
    k_dec = jnp.exp(log_g[:, None] * (c - 1.0 - idx))[:, :, None]
    chunk_dec = jnp.exp(log_g * c)[:, None, None]

    def to_chunks(t):
        return t.reshape(b, h, n, c, t.shape[-1]).transpose(2, 0, 1, 3, 4)

    def step(state, inp):
        qi, ki, vi = inp
        sc = jnp.einsum('bhqd,bhkd->bhqk', qi, ki) * inner
        o = (jnp.einsum('bhqk,bhkv->bhqv', sc, vi)
             + jnp.einsum('bhqd,bhdv->bhqv', qi, state) * q_dec)
        state = state * chunk_dec + jnp.einsum('bhkd,bhkv->bhdv', ki * k_dec, vi)
        return state, o

    state0 = jnp.zeros((b, h, d, v.shape[-1]), jnp.float32)
    _, o = lax.scan(step, state0, (to_chunks(q), to_chunks(k), to_chunks(v)))
    return o.transpose(1, 2, 0, 3, 4).reshape(b, h, s, v.shape[-1])

def head_group_norm(o, g):
    mu = jnp.mean(o, axis=-1, keepdims=True)
    var = jnp.mean(jnp.square(o - mu), axis=-1, keepdims=True)
    y = (o - mu) * lax.rsqrt(var + GN_EPS)
    return merge_heads(y) * g.astype(jnp.float32)

def moba_attention(q, k, v, rel_bias, pos):
    b, h, s, d = q.shape
    L = MOBA_BLOCK
    nb = -(-s // L)
    pad = nb * L - s
    kb = jnp.pad(k, ((0, 0), (0, 0), (0, pad), (0, 0))).reshape(b, h, nb, L, d)
    vb = jnp.pad(v, ((0, 0), (0, 0), (0, pad), (0, 0))).reshape(b, h, nb, L, d)
    kmean = jnp.mean(kb, axis=3)
    topk = min(MOBA_TOPK, nb)
    scale = d ** -0.5
    bias_t = rel_bias.astype(jnp.float32).T
    qc_len = MOBA_Q_CHUNK
    n_qc = s // qc_len
    qc = q.reshape(b, h, n_qc, qc_len, d).transpose(2, 0, 1, 3, 4)
    bi = jnp.arange(b)[:, None, None, None]
    hi = jnp.arange(h)[None, :, None, None]
    blk_ids = jnp.arange(nb)
    offs = jnp.arange(L)

    def one_chunk(args):
        qi, ci = args
        q_pos = pos[0] + ci * qc_len + jnp.arange(qc_len)
        own = (ci * qc_len) // L
        gate = jnp.einsum('bhqd,bhnd->bhqn', qi, kmean)
        gate = jnp.where(blk_ids < own, gate, -jnp.inf)
        _, sel = lax.top_k(gate, topk)
        valid = sel < own
        ks = kb[bi, hi, sel]
        vs = vb[bi, hi, sel]
        s_sel = jnp.einsum('bhqd,bhqnld->bhqnl', qi, ks) * scale
        k_pos_sel = pos[0] + sel[..., None] * L + offs
        rel_sel = q_pos[None, None, :, None, None] - k_pos_sel
        s_sel = s_sel + bias_t[hi[..., None], t5_bucket(rel_sel)]
        s_sel = jnp.where(valid[..., None], s_sel, NEG).reshape(b, h, qc_len, topk * L)
        k_own = lax.dynamic_slice_in_dim(kb, own, 1, axis=2)[:, :, 0]
        v_own = lax.dynamic_slice_in_dim(vb, own, 1, axis=2)[:, :, 0]
        rel_own = q_pos[:, None] - (pos[0] + own * L + offs)[None, :]
        s_own = jnp.einsum('bhqd,bhld->bhql', qi, k_own) * scale + bias_t[:, t5_bucket(rel_own)]
        s_own = jnp.where(rel_own >= 0, s_own, NEG)
        p = jax.nn.softmax(jnp.concatenate([s_sel, s_own], axis=-1), axis=-1)
        p_sel = p[..., : topk * L].reshape(b, h, qc_len, topk, L)
        p_own = p[..., topk * L:]
        return (jnp.einsum('bhqnl,bhqnld->bhqd', p_sel, vs)
                + jnp.einsum('bhql,bhld->bhqd', p_own, v_own))

    o = lax.map(one_chunk, (qc, jnp.arange(n_qc)))
    return o.transpose(1, 2, 0, 3, 4).reshape(b, h, s, d)

def forgetting_attention(q, k, v, log_f):
    b, h, s, d = q.shape
    qb_len = FOX_Q_BLOCK
    n_qb = s // qb_len
    scale = d ** -0.5
    F = jnp.cumsum(log_f, axis=-1)
    qb = q.reshape(b, h, n_qb, qb_len, d).transpose(2, 0, 1, 3, 4)
    Fb = F.reshape(b, h, n_qb, qb_len).transpose(2, 0, 1, 3)
    k_pos = jnp.arange(s)

    def one_block(args):
        qi, Fi, blk = args
        q_pos = blk * qb_len + jnp.arange(qb_len)
        sc = (jnp.einsum('bhqd,bhkd->bhqk', qi, k) * scale
              + Fi[..., :, None] - F[:, :, None, :])
        sc = jnp.where(k_pos[None, :] <= q_pos[:, None], sc, NEG)
        p = jax.nn.softmax(sc, axis=-1)
        return jnp.einsum('bhqk,bhkd->bhqd', p, v)

    o = lax.map(one_block, (qb, Fb, jnp.arange(n_qb)))
    return o.transpose(1, 2, 0, 3, 4).reshape(b, h, s, d)

def even_mixer(h, w_in, gn_w, w_out, rel_bias, pos):
    proj = h @ w_in
    cuts = [RET_WIDTH * i for i in range(1, 5)] + [4 * RET_WIDTH + MOBA_WIDTH * i for i in range(1, 3)]
    rq, rk, rv, rg, mq, mk, mv = jnp.split(proj, cuts, axis=-1)
    ret = retention(split_heads(rq, RET_HEADS), split_heads(rk, RET_HEADS),
                    split_heads(rv, RET_HEADS), pos)
    ret = head_group_norm(ret, gn_w) * jax.nn.silu(rg.astype(jnp.float32))
    mob = merge_heads(moba_attention(split_heads(mq, MOBA_HEADS), split_heads(mk, MOBA_HEADS),
                                     split_heads(mv, MOBA_HEADS), rel_bias, pos))
    cat = jnp.concatenate([ret, mob], axis=-1).astype(h.dtype)
    return cat @ w_out

def odd_mixer(h, w_in, b_forget, w_out):
    proj = h @ w_in
    fq, fk, fv, fl = jnp.split(proj, [FOX_WIDTH, 2 * FOX_WIDTH, 3 * FOX_WIDTH], axis=-1)
    log_f = jax.nn.log_sigmoid(fl.astype(jnp.float32) + b_forget.astype(jnp.float32))
    o = forgetting_attention(split_heads(fq, FOX_HEADS), split_heads(fk, FOX_HEADS),
                             split_heads(fv, FOX_HEADS), log_f.transpose(0, 2, 1))
    return merge_heads(o).astype(h.dtype) @ w_out

def swiglu(h, w_in, w_out):
    gu = h @ w_in
    g, u = jnp.split(gu, [FFN_HIDDEN], axis=-1)
    return (jax.nn.silu(g) * u) @ w_out

def setup_inputs(seed: int = 0) -> dict:
    key = jax.random.key(seed)
    ks = jax.random.split(key, 15)
    f32 = jnp.float32

    def w(k, shape, fan_in):
        return jax.random.normal(k, shape, f32) * (fan_in ** -0.5)

    def gain(k, shape):
        return 1.0 + 0.05 * jax.random.normal(k, shape, f32)

    return {
        "x": jax.random.normal(ks[0], (BATCH, SEQ, D_MODEL), f32),
        "rel_bias": 0.5 * jax.random.normal(ks[1], (N_REL_BUCKETS, MOBA_HEADS), f32),
        "norm_mix_pre": gain(ks[2], (DEPTH, D_MODEL)),
        "norm_mix_post": gain(ks[3], (DEPTH, D_MODEL)),
        "norm_ffn_pre": gain(ks[4], (DEPTH, D_MODEL)),
        "norm_ffn_post": gain(ks[5], (DEPTH, D_MODEL)),
        "even_w_in": w(ks[6], (N_EVEN, D_MODEL, EVEN_IN), D_MODEL),
        "even_gn": gain(ks[7], (N_EVEN, RET_WIDTH)),
        "even_w_out": w(ks[8], (N_EVEN, RET_WIDTH + MOBA_WIDTH, D_MODEL), RET_WIDTH + MOBA_WIDTH),
        "odd_w_in": w(ks[9], (N_ODD, D_MODEL, ODD_IN), D_MODEL),
        "odd_b_forget": 2.0 + 0.5 * jax.random.normal(ks[10], (N_ODD, FOX_HEADS), f32),
        "odd_w_out": w(ks[11], (N_ODD, FOX_WIDTH, D_MODEL), FOX_WIDTH),
        "ffn_w_in": w(ks[12], (DEPTH, D_MODEL, 2 * FFN_HIDDEN), D_MODEL),
        "ffn_w_out": w(ks[13], (DEPTH, FFN_HIDDEN, D_MODEL), FFN_HIDDEN),
    }

def reference(x, rel_bias, norm_mix_pre, norm_mix_post, norm_ffn_pre, norm_ffn_post,
              even_w_in, even_gn, even_w_out, odd_w_in, odd_b_forget, odd_w_out,
              ffn_w_in, ffn_w_out):
    pos = jnp.arange(x.shape[1], dtype=jnp.int32)
    for layer in range(DEPTH):
        i = layer // 2
        hn = rms_norm(x, norm_mix_pre[layer])
        if layer % 2 == 0:
            m = even_mixer(hn, even_w_in[i], even_gn[i], even_w_out[i], rel_bias, pos)
        else:
            m = odd_mixer(hn, odd_w_in[i], odd_b_forget[i], odd_w_out[i])
        x = x + rms_norm(m, norm_mix_post[layer])
        hn = rms_norm(x, norm_ffn_pre[layer])
        x = x + rms_norm(swiglu(hn, ffn_w_in[layer], ffn_w_out[layer]), norm_ffn_post[layer])
    return x


_drawn_inputs = setup_inputs


def setup_inputs(seed=0):
    import zlib

    import numpy as np

    out = dict(_drawn_inputs(seed))
    spreads = {}
    factors = {}
    for name, (base, spread) in spreads.items():
        noise = np.random.default_rng([zlib.crc32(name.encode()), seed]).standard_normal(out[name].shape)
        drawn = base * np.exp(spread * noise) if base else spread * noise
        out[name] = __import__('jax').numpy.asarray(drawn.astype(out[name].dtype))
    for name, factor in factors.items():
        out[name] = (out[name] * factor).astype(out[name].dtype)
    return out
```

```python
from contextlib import ExitStack

import numpy as np

import concourse.bass as bass
from concourse import mybir

F32 = mybir.dt.float32
F32R = mybir.dt.float32r
BF16 = mybir.dt.bfloat16
ALU = mybir.AluOpType
ACT = mybir.ActivationFunctionType
AX_X = mybir.AxisListType.X

P = 128
SEQ, DIM, HEAD = 512, 1024, 128
TILES = SEQ // P
KT = DIM // P
RET, MOBA, FOX = 4, 4, 8
HIDDEN = 2816
FT = HIDDEN // P
BUCKETS = 32
MOBA_BLOCK, MOBA_TOPK = 256, 3
assert SEQ // MOBA_BLOCK <= MOBA_TOPK
NEG = -1e30
RMS_EPS, GN_EPS = 1e-6, 1e-5
SCALE = HEAD ** -0.5
DIFFS = SEQ + P

RING = 4
CHUNK = 1024
QK0 = 0
RV0 = QK0 + 2 * (RET + MOBA)
MV0 = RV0 + 4
RG0 = MV0 + 4
OUT0 = RG0 + 4
FIN0 = OUT0 + 8
FOUT0 = FIN0 + 2 * FT
QK1 = FOUT0 + FT
GATE1 = QK1 + 2 * FOX
V1 = GATE1 + 1
OUT1 = V1 + 8
FIN1 = OUT1 + 8
FOUT1 = FIN1 + 2 * FT
N_CHUNKS = FOUT1 + FT
AFTER = [QK0, FIN0, QK1, FIN1, N_CHUNKS]


def build(nc, x_in, weights, norms, gn_gain, rel_bias, forget_bias, ident_in, mask_in, decay_in,
          rotary_in, onehot_in, select_in, out):
    x_tiles = x_in.rearrange("(t p) d -> t p d", p=P)
    out_tiles = out.rearrange("(t p) d -> t p d", p=P)
    bias_rows = nc.dram_tensor("bias_rows", [MOBA, P, DIFFS], F32, kind="Internal")

    with ExitStack() as ctx:
        def sb(name, shape, dt=F32):
            return ctx.enter_context(nc.sbuf_tensor(name, shape, dt))

        def sem(name):
            return ctx.enter_context(nc.semaphore(name))

        arena_at = (nc.sbuf_base + 31) // 32 * 32
        sb("arena", [P, 90 * 256 + 8])

        def arena(name, shape, kib, dt=F32):
            return nc.alloc_sbuf_tensor_at(name, shape, dt, offset=arena_at + kib * 1024)

        ret_qk = arena("ret_qk", [P, 2 * RET, SEQ], 0)
        moba_qk = arena("moba_qk", [P, 2 * MOBA, SEQ], 16)
        ret_v = arena("ret_v", [P, TILES, RET * HEAD], 32)
        moba_v = arena("moba_v", [P, TILES, MOBA * HEAD], 40)
        ret_gate = arena("ret_gate", [P, TILES, RET * HEAD], 48)
        decay = arena("decay", [P, RET, SEQ], 56)
        rel = arena("rel", [P, MOBA, SEQ], 64)
        gn = arena("gn", [P, RET * HEAD], 72)
        probs_t = arena("probs_t", [P, 2, TILES, SEQ], 74)
        rotary = arena("rotary", [P, 2, SEQ], 74)
        turned = arena("turned", [P, SEQ], 78)
        onehot = arena("onehot", [P, DIFFS], 80)
        bias_row = arena("bias_row", [P, DIFFS], 83)
        rel_table = arena("rel_table", [P, MOBA], 86)
        fox_qk = arena("fox_qk", [P, 2 * FOX, SEQ], 0)
        fox_v = arena("fox_v", [P, TILES, FOX * HEAD], 32)
        minus_f = arena("minus_f", [P, FOX, SEQ], 48)
        select = arena("select", [P, FOX * P], 74)
        gate_work = arena("gate_work", [P, 5, SEQ], 78)
        prod_hi = arena("prod_hi", [P, FT, SEQ], 0, F32R)
        prod_lo = arena("prod_lo", [P, FT, SEQ], 44, F32R)

        x = sb("x", [P, TILES, DIM])
        h_hi = sb("h_hi", [P, KT, SEQ], F32R)
        h_lo = sb("h_lo", [P, KT, SEQ], F32R)
        w_raw = sb("w_raw", [P, RING, CHUNK])
        w_hi = sb("w_hi", [P, RING, CHUNK], F32R)
        w_lo = sb("w_lo", [P, RING, CHUNK], F32R)
        gain_post = sb("gain_post", [P, DIM])
        gain_pre = sb("gain_pre", [P, DIM])
        work = sb("work", [P, 4, SEQ])
        squares = sb("squares", [P, DIM], BF16)
        ident = sb("ident", [P, P])
        masks = sb("masks", [P, 2 * P], BF16)
        sum_post, rstd_post = sb("sum_post", [P, 16]), sb("rstd_post", [P, 16])
        sum_pre, rstd_pre = sb("sum_pre", [P, 16]), sb("rstd_pre", [P, 16])
        minus_half = sb("minus_half", [P, 4])
        gn_mean, gn_sum, gn_rstd = (sb(n, [P, 4 * RET]) for n in ("gn_mean", "gn_sum", "gn_rstd"))
        units = TILES * (MOBA + FOX)
        minus_max, row_sum, row_rec = (sb(n, [P, units]) for n in ("minus_max", "row_sum", "row_rec"))
        forget_b = sb("forget_b", [P, 1])

        ps = ctx.enter_context(nc.psum_tensor("ps", [P, 8, SEQ], F32))

        raw_landed = [sem(f"raw_landed{i}") for i in range(RING)]
        hi_done, lo_done, chunk_used = sem("hi_done"), sem("lo_done"), sem("chunk_used")
        x_landed = [sem(f"x_landed{t}") for t in range(TILES)]
        ident_landed, tables_landed = sem("ident_landed"), sem("tables_landed")
        rel_in_landed, rotary_landed = sem("rel_in_landed"), sem("rotary_landed")
        gain_pre_landed, gain_post_landed = sem("gain_pre_landed"), sem("gain_post_landed")
        select_landed = sem("select_landed")
        y_done, post_summed, post_rstd, x_updated = (
            sem(n) for n in ("y_done", "post_summed", "post_rstd", "x_updated"))
        pre_summed, pre_rstd, normed, h_turned, h_hi_done, h_ready = (
            sem(n) for n in ("pre_summed", "pre_rstd", "normed", "h_turned", "h_hi_done", "h_ready"))
        evacuated, turned_parts = sem("evacuated"), sem("turned_parts")
        gate_done = sem("gate_done")
        rel_rows_done, rel_copied, rel_stored, rel_landed = (
            sem(n) for n in ("rel_rows_done", "rel_copied", "rel_stored", "rel_landed"))
        forget_logit, forget_log, f_ready, f_spread = (
            sem(n) for n in ("forget_logit", "forget_log", "f_ready", "f_spread"))
        ret_scored, ret_decayed, ret_out, ret_centred, ret_squared, ret_summed, ret_rstd, ret_y = (
            sem(n) for n in ("ret_scored", "ret_decayed", "ret_out", "ret_centred", "ret_squared",
                             "ret_summed", "ret_rstd", "ret_y"))
        scored, logits, exped, probs, probs_turned, probs_t_ready = (
            sem(n) for n in ("scored", "logits", "exped", "probs", "probs_turned", "probs_t_ready"))
        head_done, head_hi, head_ready = sem("head_done"), sem("head_hi"), sem("head_ready")
        silu_done, product_done, product_hi, product_ready = (
            sem(n) for n in ("silu_done", "product_done", "product_hi", "product_ready"))
        vec_step, act_step, pool_step = sem("vec_step"), sem("act_step"), sem("pool_step")
        stored = sem("stored")

        block = ctx.enter_context(nc.Block())

        def cols(t, n=1):
            return slice(t * P, (t + n) * P)

        @block.sync
        def _(sp):
            for t in range(TILES):
                sp.dma_start(x[:, t], x_tiles[t]).then_inc(x_landed[t], 16)
            for c in range(RING):
                sp.dma_start(w_raw[:, c], weights[c]).then_inc(raw_landed[c], 16)
            groups = N_CHUNKS // RING
            with nc.sync.Fori(1, groups) as g:
                for i in range(RING):
                    sp.wait_ge(lo_done, g * RING + (i + 1 - RING))
                    sp.dma_start(w_raw[:, i], weights[g * RING + i]).then_inc(raw_landed[i], 16)
            for c in range(groups * RING, N_CHUNKS):
                sp.wait_ge(lo_done, c + 1 - RING)
                sp.dma_start(w_raw[:, c % RING], weights[c]).then_inc(raw_landed[c % RING], 16)
            for t in range(TILES):
                sp.wait_ge(x_updated, 4 * 3 + t + 1)
                sp.dma_start(out_tiles[t], x[:, t]).then_inc(stored, 16)
            sp.wait_ge(stored, 16 * TILES)

        @block.gpsimd
        def _(pool):
            steps = [0]

            def low(c, group=0):
                pool.wait_ge(hi_done, group * RING + (c + 1))
                nc.gpsimd.tensor_tensor(w_lo[:, c % RING], w_raw[:, c % RING],
                                        w_hi[:, c % RING].bitcast(F32), ALU.subtract).then_inc(lo_done, 1)

            def lows(c0, c1):
                n = (c1 - c0) // RING
                if n > 1:
                    with nc.gpsimd.Fori(0, n) as g:
                        for i in range(RING):
                            low(c0 + i, g)
                    c0 += n * RING
                for c in range(c0, c1):
                    low(c)

            def own(ins):
                steps[0] += 1
                ins.then_inc(pool_step, 1)
                pool.wait_ge(pool_step, steps[0])

            def rstd(to, of, size, eps, done):
                own(nc.gpsimd.tensor_scalar(of, of, 1.0 / size, eps, ALU.mult, ALU.add))
                nc.gpsimd.tensor_tensor(to, of, minus_half[:, 0:of.shape[1]], ALU.pow).then_inc(done, 1)

            def boundary(b, tiles):
                if b:
                    for t in tiles:
                        q = 4 * (b - 1) + t
                        pool.wait_ge(post_summed, q + 1)
                        rstd(rstd_post[:, q:q + 1], sum_post[:, q:q + 1], DIM, RMS_EPS, post_rstd)
                if b < 4:
                    for t in tiles:
                        q = 4 * b + t
                        pool.wait_ge(pre_summed, q + 1)
                        rstd(rstd_pre[:, q:q + 1], sum_pre[:, q:q + 1], DIM, RMS_EPS, pre_rstd)

            own(nc.gpsimd.memset(minus_half[:], -0.5))
            boundary(0, (0, 1))
            lows(0, RING)
            boundary(0, (2, 3))
            lows(RING, OUT0 + RING)
            for h in range(RET):
                pool.wait_ge(ret_summed, h + 1)
                rstd(gn_rstd[:, 4 * h:4 * h + 4], gn_sum[:, 4 * h:4 * h + 4], HEAD, GN_EPS, ret_rstd)
            at = OUT0 + RING
            for b in range(1, 4):
                lows(at, AFTER[b])
                boundary(b, (0, 1))
                lows(AFTER[b], AFTER[b] + RING)
                boundary(b, (2, 3))
                at = AFTER[b] + RING
            lows(at, N_CHUNKS)
            boundary(4, (0, 1))
            boundary(4, (2, 3))

        @block.scalar
        def _(act):
            steps = [0]

            def own(ins):
                steps[0] += 1
                ins.then_inc(act_step, 1)
                act.wait_ge(act_step, steps[0])

            def high(c, group=0):
                if c >= RING:
                    act.wait_ge(chunk_used, group * RING + (c + 1 - RING))
                act.wait_ge(raw_landed[c % RING], group * 16 + 16 * (c // RING + 1))
                nc.scalar.activation(w_hi[:, c % RING], w_raw[:, c % RING], ACT.Copy).then_inc(hi_done, 1)

            def highs(c0, c1):
                n = (c1 - c0) // RING
                if n > 1:
                    with nc.scalar.Fori(0, n) as g:
                        for i in range(RING):
                            high(c0 + i, g)
                    c0 += n * RING
                for c in range(c0, c1):
                    high(c)

            def sum_post_squares(b, t):
                q = 4 * (b - 1) + t
                if t < 3:
                    act.wait_ge(y_done, 3 * (b - 1) + t + 1)
                else:
                    act.wait_ge(chunk_used, AFTER[b])
                if t:
                    act.wait_ge(post_summed, q)
                nc.scalar.activation(squares[:], ps[:, 2 * t:2 * t + 2, :], ACT.Square,
                                     accum_out=sum_post[:, q:q + 1]).then_inc(post_summed, 1)

            def sum_pre_squares(b, t):
                q = 4 * b + t
                if b:
                    act.wait_ge(x_updated, q - 3)
                else:
                    act.wait_ge(x_landed[t], 16)
                if t % 2:
                    act.wait_ge(pre_summed, q)
                elif b:
                    act.wait_ge(post_summed, 4 * (b - 1) + t + 2)
                nc.scalar.activation(squares[:], x[:, t], ACT.Square,
                                     accum_out=sum_pre[:, q:q + 1]).then_inc(pre_summed, 1)

            def turned_high(b, t):
                act.wait_ge(h_turned, 4 * b + t + 1)
                nc.scalar.activation(h_hi[:, :, cols(t)],
                                     ps[:, 2 * t:2 * t + 2, :].rearrange("p a (k s) -> p (a k) s", s=P),
                                     ACT.Copy).then_inc(h_hi_done, 1)

            def boundary(b):
                for pair in ((0, 1), (2, 3)):
                    for t in pair:
                        if b:
                            sum_post_squares(b, t)
                    if b < 4:
                        for t in pair:
                            sum_pre_squares(b, t)
                        if pair[0] == 0:
                            highs(AFTER[b], AFTER[b] + RING)
                        for t in pair:
                            turned_high(b, t)
                if b < 3:
                    act.wait_ge(normed, 4 * b + 4)
                    act.dma_start(gain_pre[:], norms[b + 1, 0].partition_broadcast(P)).then_inc(gain_pre_landed, 16)
                if 0 < b < 4:
                    act.wait_ge(x_updated, 4 * b)
                    act.dma_start(gain_post[:], norms[b, 1].partition_broadcast(P)).then_inc(gain_post_landed, 16)

            def head_high(hd):
                act.wait_ge(head_done, hd + 1)
                nc.scalar.activation(h_hi[:, hd % KT, :], ps[:, 5 + 2 * (hd % 2), :], ACT.Copy).then_inc(head_hi, 1)

            def attention(heads, unit0, head0):
                n_units = TILES * heads
                for n in range(n_units + 6):
                    if n < n_units:
                        u, i = unit0 + n, n % TILES
                        act.wait_ge(logits, u + 1)
                        nc.scalar.activation(work[:, n % 4, 0:(i + 1) * P], work[:, n % 4, 0:(i + 1) * P],
                                             ACT.Exp, bias=minus_max[:, u:u + 1], scale=-1.0,
                                             accum_out=row_sum[:, u:u + 1]).then_inc(exped, 1)
                    m = n - 3
                    if 0 <= m < n_units:
                        h, i, u = m // TILES, m % TILES, unit0 + m
                        act.wait_ge(probs_turned, u + 1)
                        if h >= 2:
                            act.wait_ge(head_done, head0 + h - 1)
                        nc.scalar.activation(probs_t[:, h % 2, 0:i + 1, cols(i)],
                                             ps[:, 4 + 2 * (u % 2), 0:(i + 1) * P].rearrange("p (j q) -> p j q", q=P),
                                             ACT.Copy).then_inc(probs_t_ready, 1)
                    m = n - 5
                    if m >= 0 and m % TILES == 3 and m < n_units:
                        head_high(head0 + m // TILES)

            def ffn(c0, tile0):
                def pair(p, gate_bank, group=0, step=0):
                    at = group * step
                    high(c0 + RING + 2 * p, group if step else 0)
                    high(c0 + RING + 2 * p + 1, group if step else 0)
                    act.wait_ge(chunk_used, group * RING * bool(step) + (c0 + 2 * p + 2))
                    if tile0 + p >= 2:
                        act.wait_ge(product_done, at + (tile0 + p - 1))
                    nc.scalar.activation(work[:, p % 2, :], ps[:, gate_bank, :], ACT.Silu).then_inc(silu_done, 1)
                    act.wait_ge(product_done, at + (tile0 + p + 1))
                    nc.scalar.activation(prod_hi[:, at + p, :] if step else prod_hi[:, p, :],
                                         work[:, 2 + p % 2, :], ACT.Copy).then_inc(product_hi, 1)

                pair(0, 0)
                pair(1, 2)
                with nc.scalar.Fori(0, (FT - 2) // 2) as g:
                    pair(2, 1, g, 2)
                    pair(3, 5, g, 2)

            act.dma_start(ident[:], ident_in).then_inc(ident_landed, 16)
            act.dma_start(gain_pre[:], norms[0, 0].partition_broadcast(P)).then_inc(gain_pre_landed, 16)
            act.dma_start(rotary[:], rotary_in).then_inc(rotary_landed, 16)
            act.dma_start(onehot[0:BUCKETS + 1, :], onehot_in).then_inc(rel_in_landed, 16)
            act.dma_start(rel_table[0:BUCKETS + 1, :], rel_bias).then_inc(rel_in_landed, 16)
            act.dma_start(gain_post[:], norms[0, 1].partition_broadcast(P)).then_inc(gain_post_landed, 16)
            act.dma_start(decay[:], decay_in).then_inc(tables_landed, 16)
            act.dma_start(gn[:], gn_gain.partition_broadcast(P)).then_inc(tables_landed, 16)
            act.dma_start(masks[:], mask_in).then_inc(tables_landed, 16)
            act.dma_start(forget_b[0:FOX, :], forget_bias).then_inc(tables_landed, 16)

            boundary(0)
            highs(QK0 + RING, QK0 + 3 * RING)
            act.wait_ge(rel_copied, 1)
            act.dma_start(bias_rows.ap(), bias_row[0:MOBA, :].unsqueeze(1).to_broadcast([MOBA, P, DIFFS])).then_inc(rel_stored, 16)
            highs(QK0 + 3 * RING, RV0 + RING)
            act.wait_ge(rel_stored, 16)
            act.dma_start(rel[:], bass.AP(bias_rows, P - 1, [[DIFFS - 1, P], [P * DIFFS, MOBA], [1, SEQ]])).then_inc(rel_landed, 16)
            highs(RV0 + RING, OUT0 + RING)
            act.wait_ge(chunk_used, OUT0)
            for t in range(TILES):
                nc.scalar.activation(ret_gate[:, t, :], ps[:, 4 + t, :], ACT.Silu).then_inc(gate_done, 1)
            for s in range(RET + 3):
                if 1 <= s <= RET:
                    h = s - 1
                    act.wait_ge(ret_centred, h + 1)
                    nc.scalar.activation(work[:, 2, :], work[:, h % 2, :], ACT.Square).then_inc(ret_squared, 1)
                    act.wait_ge(ret_summed, h + 1)
                if s >= 3:
                    head_high(s - 3)
            attention(MOBA, 0, RET)
            highs(OUT0 + RING, FIN0)
            boundary(1)
            ffn(FIN0, 0)
            highs(FOUT0 + RING, QK1)
            boundary(2)
            act.dma_start(select[0:FOX, :], select_in).then_inc(select_landed, 16)
            highs(QK1 + RING, GATE1 + RING + 1)
            act.wait_ge(forget_logit, 1)
            own(nc.scalar.activation(gate_work[0:FOX, 3, :], gate_work[0:FOX, 2, :], ACT.Exp))
            nc.scalar.activation(gate_work[0:FOX, 2, :], gate_work[0:FOX, 3, :], ACT.Ln, bias=1.0).then_inc(forget_log, 1)
            highs(GATE1 + RING + 1, OUT1 + RING)
            attention(FOX, TILES * MOBA, KT)
            highs(OUT1 + RING, FIN1)
            boundary(3)
            ffn(FIN1, FT)
            highs(FOUT1 + RING, N_CHUNKS)
            boundary(4)

        @block.vector
        def _(vec):
            steps = [0]

            def own(ins):
                steps[0] += 1
                ins.then_inc(vec_step, 1)
                vec.wait_ge(vec_step, steps[0])

            def post(b, t):
                q = 4 * (b - 1) + t
                row = work[:, 2 * (t % 2):2 * (t % 2) + 2, :].rearrange("p a s -> p (a s)")
                vec.wait_ge(gain_post_landed, 16 * b)
                vec.wait_ge(post_rstd, q + 1)
                if t >= 2:
                    vec.wait_ge(x_updated, q - 1)
                    if b < 4:
                        vec.wait_ge(h_turned, 4 * b + t - 1)
                own(nc.vector.scalar_tensor_tensor(
                    out=row, in0=ps[:, 2 * t:2 * t + 2, :].rearrange("p a s -> p (a s)"),
                    scalar=rstd_post[:, q:q + 1], in1=gain_post[:], op0=ALU.mult, op1=ALU.mult))
                nc.vector.tensor_tensor(x[:, t], x[:, t], row, ALU.add).then_inc(x_updated, 1)

            def pre(b, t):
                q = 4 * b + t
                row = work[:, 2 * (t % 2):2 * (t % 2) + 2, :].rearrange("p a s -> p (a s)")
                vec.wait_ge(gain_pre_landed, 16 * (b + 1))
                vec.wait_ge(pre_rstd, q + 1)
                if b:
                    vec.wait_ge(x_updated, q - 3)
                elif t >= 2:
                    vec.wait_ge(h_turned, q - 1)
                nc.vector.scalar_tensor_tensor(
                    out=row, in0=x[:, t], scalar=rstd_pre[:, q:q + 1], in1=gain_pre[:],
                    op0=ALU.mult, op1=ALU.mult).then_inc(normed, 1)

            def turned_low(b, t):
                vec.wait_ge(h_hi_done, 4 * b + t + 1)
                nc.vector.tensor_tensor(
                    h_lo[:, :, cols(t)], ps[:, 2 * t:2 * t + 2, :].rearrange("p a (k s) -> p (a k) s", s=P),
                    h_hi[:, :, cols(t)].bitcast(F32), ALU.subtract).then_inc(h_ready, 1)

            def boundary(b):
                if b in (2, 4):
                    vec.wait_ge(product_ready, FT * b // 2)
                for pair in ((0, 1), (2, 3)):
                    for t in pair:
                        if b:
                            post(b, t)
                    if b < 4:
                        for t in pair:
                            pre(b, t)
                        for t in pair:
                            turned_low(b, t)

            def evacuate(to, bank, scale=None):
                if scale is None:
                    ins = nc.vector.tensor_copy(to, ps[:, bank, :])
                else:
                    ins = nc.vector.tensor_scalar(to, ps[:, bank, :], scale, None, ALU.mult)
                ins.then_inc(evacuated, 1)

            def head_low(hd):
                vec.wait_ge(head_hi, hd + 1)
                nc.vector.tensor_tensor(h_lo[:, hd % KT, :], ps[:, 5 + 2 * (hd % 2), :],
                                        h_hi[:, hd % KT, :].bitcast(F32), ALU.subtract).then_inc(head_ready, 1)

            def attention(heads, unit0, head0, table):
                n_units = TILES * heads
                for n in range(n_units + 7):
                    if n < n_units:
                        u, h, i = unit0 + n, n // TILES, n % TILES
                        vec.wait_ge(scored, u + 1)
                        if n >= 4:
                            vec.wait_ge(probs_turned, u - 3)
                        nc.vector.tensor_tensor_reduce(
                            work[:, n % 4, 0:(i + 1) * P], ps[:, u % 4, 0:(i + 1) * P], table(h, i),
                            -1.0, float(np.finfo(np.float32).max), ALU.add, ALU.min,
                            minus_max[:, u:u + 1]).then_inc(logits, 1)
                    m = n - 1
                    if 0 <= m < n_units:
                        u, i = unit0 + m, m % TILES
                        vec.wait_ge(exped, u + 1)
                        own(nc.vector.reciprocal(row_rec[:, u:u + 1], row_sum[:, u:u + 1]))
                        nc.vector.tensor_scalar(work[:, m % 4, 0:(i + 1) * P], work[:, m % 4, 0:(i + 1) * P],
                                                row_rec[:, u:u + 1], None, ALU.mult).then_inc(probs, 1)
                    m = n - 6
                    if m >= 0 and m % TILES == 3:
                        head_low(head0 + m // TILES)

            def ffn(c0, tile0):
                def pair(p, up_bank, group=0, step=0):
                    at = group * step
                    vec.wait_ge(silu_done, at + (tile0 + p + 1))
                    if tile0 + p >= 2:
                        vec.wait_ge(product_ready, at + (tile0 + p - 1))
                    nc.vector.tensor_tensor(work[:, 2 + p % 2, :], work[:, p % 2, :], ps[:, up_bank, :],
                                            ALU.mult).then_inc(product_done, 1)
                    vec.wait_ge(product_hi, at + (tile0 + p + 1))
                    tile = at + p if step else p
                    nc.vector.tensor_tensor(prod_lo[:, tile, :], work[:, 2 + p % 2, :],
                                            prod_hi[:, tile, :].bitcast(F32), ALU.subtract).then_inc(product_ready, 1)

                pair(0, 1)
                pair(1, 3)
                with nc.vector.Fori(0, (FT - 2) // 2) as g:
                    pair(2, 3, g, 2)
                    pair(3, 7, g, 2)

            vec.wait_ge(rel_rows_done, 2)
            nc.vector.tensor_copy(bias_row[0:MOBA, :].rearrange("h (a s) -> h a s", a=2),
                                  ps[0:MOBA, 6:8, 0:DIFFS // 2]).then_inc(rel_copied, 1)
            boundary(0)
            vec.wait_ge(rotary_landed, 16)
            for i in range(2 * RET):
                vec.wait_ge(chunk_used, QK0 + i + 1)
                to, bank = ret_qk[:, i, :], ps[:, i % 4, :]
                nc.vector.tensor_tensor(to, bank, rotary[:, 0, :], ALU.mult).then_inc(turned_parts, 1)
                if i:
                    vec.wait_ge(evacuated, i)
                nc.vector.tensor_tensor(turned[0:64, :], ps[64:128, i % 4, :], rotary[64:128, 1, :],
                                        ALU.mult).then_inc(turned_parts, 1)
                nc.vector.tensor_tensor(turned[64:128, :], ps[0:64, i % 4, :], rotary[0:64, 1, :],
                                        ALU.mult).then_inc(turned_parts, 1)
                vec.wait_ge(turned_parts, 3 * (i + 1))
                nc.vector.tensor_tensor(to, to, turned[:], ALU.add).then_inc(evacuated, 1)
            for i in range(2 * MOBA):
                vec.wait_ge(chunk_used, QK0 + 2 * RET + i + 1)
                evacuate(moba_qk[:, i, :], i % 4, SCALE if i < MOBA else None)
            vec.wait_ge(chunk_used, MV0)
            for t in range(TILES):
                evacuate(ret_v[:, t, :], 4 + t)
            vec.wait_ge(chunk_used, RG0)
            for t in range(TILES):
                evacuate(moba_v[:, t, :], t)
            vec.wait_ge(tables_landed, 16 * 4)
            vec.wait_ge(rel_landed, 16)
            for s in range(RET + 4):
                if s < RET:
                    for j in range(TILES):
                        vec.wait_ge(ret_scored, 4 * s + j + 1)
                        if s >= 2:
                            vec.wait_ge(ret_out, s - 1)
                        nc.vector.tensor_tensor(probs_t[:, s % 2, j, 0:SEQ - j * P], ps[:, j, 0:SEQ - j * P],
                                                decay[:, s, 0:SEQ - j * P], ALU.mult).then_inc(ret_decayed, 1)
                if s == 0:
                    for t in range(TILES):
                        vec.wait_ge(gate_done, t + 1)
                        own(nc.vector.tensor_tensor(ret_gate[:, t, :], ret_gate[:, t, :], gn[:], ALU.mult))
                if 1 <= s <= RET:
                    h = s - 1
                    bank = ps[:, 4 + 2 * (h % 2), :].rearrange("p (t d) -> p t d", d=HEAD)
                    y = work[:, h % 2, :].rearrange("p (t d) -> p t d", d=HEAD)
                    mean, total, rstd = (a[:, 4 * h:4 * h + 4] for a in (gn_mean, gn_sum, gn_rstd))
                    vec.wait_ge(ret_out, h + 1)
                    if h >= 2:
                        vec.wait_ge(head_done, h - 1)
                    own(nc.vector.tensor_reduce(mean, bank, AX_X, ALU.add))
                    own(nc.vector.tensor_scalar(mean, mean, 1.0 / HEAD, None, ALU.mult))
                    nc.vector.tensor_tensor(y, bank, mean.unsqueeze(2).to_broadcast([P, TILES, HEAD]),
                                            ALU.subtract).then_inc(ret_centred, 1)
                    vec.wait_ge(ret_centred, h + 1)
                    vec.wait_ge(ret_squared, h + 1)
                    nc.vector.tensor_reduce(total, work[:, 2, :].rearrange("p (t d) -> p t d", d=HEAD),
                                            AX_X, ALU.add).then_inc(ret_summed, 1)
                    vec.wait_ge(ret_rstd, h + 1)
                    own(nc.vector.tensor_tensor(y, y, rstd.unsqueeze(2).to_broadcast([P, TILES, HEAD]), ALU.mult))
                    nc.vector.tensor_tensor(y, y, ret_gate[:, :, h * HEAD:(h + 1) * HEAD], ALU.mult).then_inc(ret_y, 1)
                if s >= 4:
                    head_low(s - 4)
            attention(MOBA, 0, RET, lambda h, i: rel[:, h, (TILES - 1 - i) * P:SEQ])
            boundary(1)
            ffn(FIN0, 0)
            boundary(2)
            first = 2 * (RET + MOBA) + 2 * TILES
            for scale, g0 in ((SCALE, 0), (None, FOX // 4)):
                with nc.vector.Fori(g0, g0 + FOX // 4) as g:
                    for i in range(4):
                        vec.wait_ge(chunk_used, g * 4 + (QK1 + i + 1))
                        evacuate(fox_qk[:, g * 4 + i, :], i, scale)
            z, low, neg, one, total = (gate_work[0:FOX, n, :] for n in range(5))
            vec.wait_ge(chunk_used, GATE1 + 1)
            own(nc.vector.tensor_scalar(z, ps[0:FOX, 4, :], forget_b[0:FOX, :], None, ALU.add))
            own(nc.vector.tensor_scalar(low, z, 0.0, None, ALU.min))
            nc.vector.scalar_tensor_tensor(out=neg, in0=low, scalar=2.0, in1=z, op0=ALU.mult,
                                           op1=ALU.subtract).then_inc(forget_logit, 1)
            vec.wait_ge(forget_log, 1)
            own(nc.vector.tensor_tensor(z, low, neg, ALU.subtract))
            own(nc.vector.memset(one, 1.0))
            nc.vector.tensor_tensor_scan(total, one, z, 0.0, ALU.mult, ALU.add).then_inc(f_ready, 1)
            for half in range(2):
                vec.wait_ge(chunk_used, V1 + 4 * (half + 1))
                for t in range(TILES):
                    evacuate(fox_v[:, t, half * SEQ:(half + 1) * SEQ], 4 * half + t)
            for h in range(FOX):
                vec.wait_ge(f_spread, h + 1)
                evacuate(minus_f[:, h, :], h)
            attention(FOX, TILES * MOBA, KT, lambda h, i: minus_f[:, h, 0:(i + 1) * P])
            boundary(3)
            ffn(FIN1, FT)
            boundary(4)

        @block.tensor
        def _(pe):
            mm = nc.tensor.matmul

            def exact(to, held, moved, start, stop):
                mm(to, held[0], moved[0], start=start, stop=False)
                mm(to, held[0], moved[1], start=False, stop=False)
                return mm(to, held[1], moved[0], start=False, stop=stop)

            def column_chunk(c, bank, at=slice(0, SEQ)):
                for k in range(KT):
                    last = exact(ps[:, bank, at], [w[:, c % RING, cols(k)] for w in (w_hi, w_lo)],
                                 [h[:, k, at] for h in (h_hi, h_lo)], k == 0, k == KT - 1)
                return last

            def row_chunk(c, k0, n_k, banks, tiles=range(TILES), source=(h_hi, h_lo)):
                for kk in range(2):
                    k = k0 + kk
                    for t in tiles:
                        last = exact(ps[:, banks[t], :], [s[:, k, cols(t)] for s in source],
                                     [w[:, c % RING, kk * SEQ:(kk + 1) * SEQ] for w in (w_hi, w_lo)],
                                     k == 0, k == n_k - 1)
                return last

            def turn(b, t):
                pe.wait_ge(normed, 4 * b + t + 1)
                for k in range(KT):
                    last = nc.tensor.transpose(ps[:, 2 * t + k // 4, cols(k % 4)],
                                               work[:, 2 * (t % 2) + k // 4, cols(k % 4)], ident[:])
                last.then_inc(h_turned, 1)

            def first_columns(b):
                c0 = AFTER[b]
                turn(b, 0)
                turn(b, 1)
                pe.wait_ge(h_ready, 4 * b + 2)
                for i in range(RING):
                    pe.wait_ge(lo_done, c0 + i + 1)
                    column_chunk(c0 + i, i, slice(0, SEQ // 2))
                turn(b, 2)
                turn(b, 3)
                pe.wait_ge(h_ready, 4 * b + 4)
                for i in range(RING):
                    column_chunk(c0 + i, i, slice(SEQ // 2, SEQ)).then_inc(chunk_used, 1)

            def rows(c0, n, n_k, banks, source=(h_hi, h_lo), ready=None, k0=0):
                for i in range(n):
                    if ready is not None:
                        ready(k0 + 2 * i + 1)
                    pe.wait_ge(lo_done, c0 + i + 1)
                    row_chunk(c0 + i, k0 + 2 * i, n_k, banks, source=source).then_inc(chunk_used, 1)

            def last_rows(c0, k0, n_k, banks, source=(h_hi, h_lo)):
                pe.wait_ge(lo_done, c0 + RING)
                for t in range(TILES):
                    for i in range(RING):
                        last = row_chunk(c0 + i, k0 + 2 * i, n_k, banks, (t,), source)
                        if t == TILES - 1:
                            last.then_inc(chunk_used, 1)
                        elif i == RING - 1:
                            last.then_inc(y_done, 1)

            halves = [[2 * t + half for t in range(TILES)] for half in range(2)]

            def project_out(c0, head0):
                def ready(k):
                    pe.wait_ge(head_ready, head0 + k + 1)
                rows(c0, 4, KT, halves[0], ready=ready)
                last_rows(c0 + 4, 0, KT, halves[1])

            def ffn(b, c_in, c_out, tile0):
                first_columns(b)
                with nc.tensor.Fori(0, (2 * FT - RING) // RING) as g:
                    for i in range(RING):
                        p = (RING + i) // 2
                        pe.wait_ge(product_done, g * 2 + (tile0 + p - 1 + i % 2))
                        pe.wait_ge(lo_done, g * RING + (c_in + RING + i + 1))
                        column_chunk((c_in + i) % RING, 2 * i + 1).then_inc(chunk_used, 1)

                def ready(k):
                    pe.wait_ge(product_ready, tile0 + k + 1)
                source = (prod_hi, prod_lo)
                rows(c_out, FT // 2, FT, halves[0], source, ready)
                rows(c_out + FT // 2, FT // 2 - RING, FT, halves[1], source)
                last_rows(c_out + FT - RING, FT - 2 * RING, FT, halves[1], source)

            def attention(heads, unit0, head0, q, k, v, masked):
                n_units = TILES * heads
                for n in range(n_units + 5):
                    if n < n_units:
                        u, h, i = unit0 + n, n // TILES, n % TILES
                        if n >= 4:
                            pe.wait_ge(logits, u - 3)
                        last = mm(ps[:, u % 4, 0:(i + 1) * P], q[:, h, cols(i)], k[:, h, 0:(i + 1) * P],
                                  start=True, stop=True)
                        if masked:
                            last = mm(ps[:, u % 4, cols(i)], masks[:, 0:P], masks[:, P:2 * P],
                                      start=False, stop=True, skip_group_check=True)
                        last.then_inc(scored, 1)
                    m = n - 3
                    if 0 <= m < n_units:
                        u, i = unit0 + m, m % TILES
                        pe.wait_ge(probs, u + 1)
                        if u >= 2:
                            pe.wait_ge(probs_t_ready, u - 1)
                        for j in range(i + 1):
                            last = nc.tensor.transpose(ps[:, 4 + 2 * (u % 2), cols(j)],
                                                       work[:, m % 4, cols(j)], ident[:])
                        last.then_inc(probs_turned, 1)
                    m = n - 4
                    if m >= 0 and m % TILES == 3:
                        h, hd = m // TILES, head0 + m // TILES
                        pe.wait_ge(probs_t_ready, unit0 + m + 1)
                        if hd >= 2:
                            pe.wait_ge(head_ready, hd - 1)
                        for j in range(TILES):
                            last = mm(ps[:, 5 + 2 * (hd % 2), j * P:SEQ], v[:, j, h * HEAD:(h + 1) * HEAD],
                                      probs_t[:, h % 2, j, j * P:SEQ], start=j == 0, stop=j == TILES - 1)
                        last.then_inc(head_done, 1)

            pe.wait_ge(rel_in_landed, 32)
            for half in range(2):
                mm(ps[0:MOBA, 6 + half, 0:DIFFS // 2], rel_table[0:BUCKETS + 1, :],
                   onehot[0:BUCKETS + 1, half * (DIFFS // 2):(half + 1) * (DIFFS // 2)],
                   start=True, stop=True).then_inc(rel_rows_done, 1)
            pe.wait_ge(ident_landed, 16)
            pe.wait_ge(rel_copied, 1)
            first_columns(0)
            with nc.tensor.Fori(1, (RV0 - QK0) // RING) as g:
                for i in range(RING):
                    pe.wait_ge(evacuated, g * RING + (i + 1 - RING))
                    pe.wait_ge(lo_done, g * RING + (QK0 + i + 1))
                    column_chunk(i, i).then_inc(chunk_used, 1)
            rows(RV0, 4, KT, [4, 5, 6, 7])
            pe.wait_ge(evacuated, RV0)
            rows(MV0, 4, KT, [0, 1, 2, 3])
            pe.wait_ge(evacuated, RV0 + TILES)
            rows(RG0, 4, KT, [4, 5, 6, 7])
            pe.wait_ge(evacuated, RV0 + 2 * TILES)
            pe.wait_ge(gate_done, TILES)
            for s in range(RET + 2):
                if s < RET:
                    for j in range(TILES):
                        if s >= 1:
                            pe.wait_ge(ret_decayed, 4 * (s - 1) + j + 1)
                        mm(ps[:, j, 0:SEQ - j * P], ret_qk[:, RET + s, cols(j)], ret_qk[:, s, j * P:SEQ],
                           start=True, stop=True).then_inc(ret_scored, 1)
                if 1 <= s <= RET:
                    h = s - 1
                    pe.wait_ge(ret_decayed, 4 * h + 4)
                    if h >= 2:
                        pe.wait_ge(ret_centred, h - 1)
                    for i in range(TILES):
                        for j in range(i + 1):
                            last = mm(ps[:, 4 + 2 * (h % 2), cols(i)], probs_t[:, h % 2, j, cols(i - j)],
                                      ret_v[:, j, h * HEAD:(h + 1) * HEAD], start=j == 0, stop=j == i)
                    last.then_inc(ret_out, 1)
                if s >= 2:
                    h = s - 2
                    pe.wait_ge(ret_y, h + 1)
                    if h >= 2:
                        pe.wait_ge(head_ready, h - 1)
                    for t in range(TILES):
                        last = nc.tensor.transpose(ps[:, 5 + 2 * (h % 2), cols(t)], work[:, h % 2, cols(t)], ident[:])
                    last.then_inc(head_done, 1)
            attention(MOBA, 0, RET, moba_qk[:, 0:MOBA], moba_qk[:, MOBA:2 * MOBA], moba_v, False)
            project_out(OUT0, 0)
            ffn(1, FIN0, FOUT0, 0)
            first = 2 * (RET + MOBA) + 2 * TILES
            first_columns(2)
            with nc.tensor.Fori(1, 2 * FOX // RING) as g:
                for i in range(RING):
                    pe.wait_ge(evacuated, g * RING + (first + i + 1 - RING))
                    pe.wait_ge(lo_done, g * RING + (QK1 + i + 1))
                    column_chunk((QK1 + i) % RING, i).then_inc(chunk_used, 1)
            pe.wait_ge(lo_done, GATE1 + 1)
            column_chunk(GATE1, 4).then_inc(chunk_used, 1)
            pe.wait_ge(evacuated, first + 2 * FOX)
            rows(V1, 4, KT, [0, 1, 2, 3])
            pe.wait_ge(f_ready, 1)
            rows(V1 + 4, 4, KT, [4, 5, 6, 7])
            pe.wait_ge(select_landed, 16)
            for h in range(FOX):
                pe.wait_ge(evacuated, first + 2 * FOX + h + 1)
                mm(ps[:, h, :], select[0:FOX, cols(h)], gate_work[0:FOX, 4, :],
                   start=True, stop=True).then_inc(f_spread, 1)
            pe.wait_ge(evacuated, first + 2 * FOX + 2 * TILES + FOX)
            attention(FOX, TILES * MOBA, KT, fox_qk[:, 0:FOX], fox_qk[:, FOX:2 * FOX], fox_v, True)
            project_out(OUT1, KT)
            ffn(3, FIN1, FOUT1, FT)


def constants():
    f32 = np.float32
    ident = np.eye(P, dtype=f32)
    mask = np.where(np.arange(P)[None, :] > np.arange(P)[:, None], NEG, 0.0)
    gap = np.arange(SEQ)[None, :] - np.arange(P)[:, None]
    log_g = np.log1p(-(2.0 ** (-5.0 - np.arange(RET))))
    decay = np.where(gap[:, None, :] >= 0, np.exp(log_g[None, :, None] * np.maximum(gap, 0)[:, None, :]), 0.0)
    inv = np.power(f32(10000.0), -np.arange(0, HEAD, 2, dtype=f32) / f32(HEAD)).astype(f32)
    angle = (np.arange(SEQ, dtype=f32)[None, :] * inv[:, None]).astype(f32).astype(np.float64)
    cos, sin = np.cos(angle), np.sin(angle)
    rotary = np.stack([np.concatenate([cos, cos]), np.concatenate([sin, -sin])], axis=1)
    rel = SEQ - 1 - np.arange(DIFFS)
    n = np.maximum(rel, 0)
    exact = BUCKETS // 2
    large = exact + (np.log(np.maximum(n, 1).astype(f32) / exact) / np.log(128 / exact)
                     * (BUCKETS - exact)).astype(np.int32)
    bucket = np.where(n < exact, n, np.minimum(large, BUCKETS - 1))
    onehot = np.zeros((BUCKETS + 1, DIFFS), f32)
    onehot[bucket, np.arange(DIFFS)] = rel >= 0
    onehot[BUCKETS] = np.where(rel < 0, NEG, 0.0)
    select = -np.repeat(np.eye(FOX, dtype=f32), P, axis=1)
    return ident, mask, (decay * SCALE).astype(f32), rotary.astype(f32), onehot, select


def column_chunks(w):
    n = w.shape[1] // P
    return w.reshape(KT, P, n, P).transpose(2, 1, 0, 3).reshape(n, P, KT * P)


def row_chunks(w):
    k, n = w.shape[0] // (2 * P), w.shape[1] // SEQ
    return w.reshape(k, 2, P, n, SEQ).transpose(3, 0, 2, 1, 4).reshape(n * k, P, 2 * SEQ)


def ffn_chunks(w_in, w_out):
    both = np.stack([column_chunks(w_in[:, :HIDDEN]), column_chunks(w_in[:, HIDDEN:])], axis=1)
    return [both.reshape(2 * FT, P, CHUNK), row_chunks(w_out)]


def kernel(x, rel_bias, norm_mix_pre, norm_mix_post, norm_ffn_pre, norm_ffn_post, even_w_in, even_gn,
           even_w_out, odd_w_in, odd_b_forget, odd_w_out, ffn_w_in, ffn_w_out):
    import concourse.bacc as bacc
    from concourse.bass_utils import run_bass_kernel_spmd
    import ml_dtypes

    a = np.asarray
    even, odd = a(even_w_in)[0], a(odd_w_in)[0]
    ffn_in, ffn_out = a(ffn_w_in), a(ffn_w_out)
    rw, mw, fw = RET * HEAD, MOBA * HEAD, FOX * HEAD
    q_and_k = np.concatenate([even[:, :2 * rw], even[:, 4 * rw:4 * rw + 2 * mw]], axis=1)
    gate = np.concatenate([odd[:, 3 * fw:], np.zeros((DIM, P - FOX), np.float32)], axis=1)
    stream = np.concatenate([
        column_chunks(q_and_k), row_chunks(even[:, 2 * rw:3 * rw]), row_chunks(even[:, 4 * rw + 2 * mw:]),
        row_chunks(even[:, 3 * rw:4 * rw]), row_chunks(a(even_w_out)[0]),
        *ffn_chunks(ffn_in[0], ffn_out[0]),
        column_chunks(odd[:, :2 * fw]), column_chunks(gate), row_chunks(odd[:, 2 * fw:3 * fw]),
        row_chunks(a(odd_w_out)[0]),
        *ffn_chunks(ffn_in[1], ffn_out[1]),
    ])
    assert stream.shape == (N_CHUNKS, P, CHUNK)
    pre = [a(norm_mix_pre)[0], a(norm_ffn_pre)[0], a(norm_mix_pre)[1], a(norm_ffn_pre)[1]]
    post = [a(norm_mix_post)[0], a(norm_ffn_post)[0], a(norm_mix_post)[1], a(norm_ffn_post)[1]]
    ident, mask, decay, rotary, onehot, select = constants()
    arrays = {
        "x_in": a(x)[0],
        "weights": stream,
        "norms": np.stack([np.stack(pre), np.stack(post)], axis=1),
        "gn_gain": a(even_gn)[0],
        "rel_bias": np.concatenate([a(rel_bias), np.ones((1, MOBA), np.float32)]),
        "forget_bias": a(odd_b_forget)[0][:, None],
        "ident_in": ident,
        "mask_in": np.concatenate([ident, mask], axis=1).astype(ml_dtypes.bfloat16),
        "decay_in": decay,
        "rotary_in": rotary,
        "onehot_in": onehot,
        "select_in": select,
    }
    nc = bacc.Bacc("TRN2", target_bir_lowering=False, num_devices=1)
    arrays = {n: np.ascontiguousarray(v) for n, v in arrays.items()}
    args = {n: nc.dram_tensor(n, v.shape, mybir.dt.from_np(v.dtype), kind="ExternalInput").ap()
            for n, v in arrays.items()}
    out = nc.dram_tensor("out", (SEQ, DIM), F32, kind="ExternalOutput").ap()
    build(nc, **args, out=out)
    result = run_bass_kernel_spmd(nc, [arrays], core_ids=[0])
    return result.results[0]["out"].reshape(1, SEQ, DIM)
```

```python
from contextlib import ExitStack

import numpy as np

import concourse.bass as bass
from concourse import mybir

F32 = mybir.dt.float32
F32R = mybir.dt.float32r
BF16 = mybir.dt.bfloat16
ALU = mybir.AluOpType
ACT = mybir.ActivationFunctionType
AX_X = mybir.AxisListType.X

P = 128
SEQ, DIM, HEAD = 512, 1024, 128
TILES = SEQ // P
KT = DIM // P
RET, MOBA, FOX = 4, 4, 8
HIDDEN = 2816
FT = HIDDEN // P
BUCKETS = 32
MOBA_BLOCK, MOBA_TOPK = 256, 3
assert SEQ // MOBA_BLOCK <= MOBA_TOPK
NEG = -1e30
RMS_EPS, GN_EPS = 1e-6, 1e-5
SCALE = HEAD ** -0.5
DIFFS = SEQ + P

RING = 4
CHUNK = 1024
QK0 = 0
RV0 = QK0 + 2 * (RET + MOBA)
MV0 = RV0 + 4
RG0 = MV0 + 4
OUT0 = RG0 + 4
FIN0 = OUT0 + 8
FOUT0 = FIN0 + 2 * FT
QK1 = FOUT0 + FT
GATE1 = QK1 + 2 * FOX
V1 = GATE1 + 1
OUT1 = V1 + 8
FIN1 = OUT1 + 8
FOUT1 = FIN1 + 2 * FT
N_CHUNKS = FOUT1 + FT
AFTER = [QK0, FIN0, QK1, FIN1, N_CHUNKS]


def build(nc, x_in, weights, norms, gn_gain, rel_bias, forget_bias, ident_in, mask_in, decay_in,
          rotary_in, onehot_in, select_in, out):
    x_tiles = x_in.rearrange("(t p) d -> t p d", p=P)
    out_tiles = out.rearrange("(t p) d -> t p d", p=P)
    bias_rows = nc.dram_tensor("bias_rows", [MOBA, P, DIFFS], F32, kind="Internal")

    with ExitStack() as ctx:
        def sb(name, shape, dt=F32):
            return ctx.enter_context(nc.sbuf_tensor(name, shape, dt))

        def sem(name):
            return ctx.enter_context(nc.semaphore(name))

        arena_at = (nc.sbuf_base + 31) // 32 * 32
        sb("arena", [P, 90 * 256 + 8])

        def arena(name, shape, kib, dt=F32):
            return nc.alloc_sbuf_tensor_at(name, shape, dt, offset=arena_at + kib * 1024)

        ret_qk = arena("ret_qk", [P, 2 * RET, SEQ], 0)
        moba_qk = arena("moba_qk", [P, 2 * MOBA, SEQ], 16)
        ret_v = arena("ret_v", [P, TILES, RET * HEAD], 32)
        moba_v = arena("moba_v", [P, TILES, MOBA * HEAD], 40)
        ret_gate = arena("ret_gate", [P, TILES, RET * HEAD], 48)
        decay = arena("decay", [P, RET, SEQ], 56)
        rel = arena("rel", [P, MOBA, SEQ], 64)
        gn = arena("gn", [P, RET * HEAD], 72)
        probs_t = arena("probs_t", [P, 2, TILES, SEQ], 74)
        rotary = arena("rotary", [P, 2, SEQ], 74)
        turned = arena("turned", [P, SEQ], 78)
        onehot = arena("onehot", [P, DIFFS], 80)
        bias_row = arena("bias_row", [P, DIFFS], 83)
        rel_table = arena("rel_table", [P, MOBA], 86)
        fox_qk = arena("fox_qk", [P, 2 * FOX, SEQ], 0)
        fox_v = arena("fox_v", [P, TILES, FOX * HEAD], 32)
        minus_f = arena("minus_f", [P, FOX, SEQ], 48)
        select = arena("select", [P, FOX * P], 74)
        gate_work = arena("gate_work", [P, 5, SEQ], 78)
        prod_hi = arena("prod_hi", [P, FT, SEQ], 0, F32R)
        prod_lo = arena("prod_lo", [P, FT, SEQ], 44, F32R)

        x = sb("x", [P, TILES, DIM])
        h_hi = sb("h_hi", [P, KT, SEQ], F32R)
        h_lo_at = (nc.sbuf_base + 31) // 32 * 32
        h_lo = sb("h_lo", [P, KT, SEQ], F32R)
        ret_y_rows = nc.alloc_sbuf_tensor_at("ret_y_rows", [P, RET, SEQ], F32, offset=h_lo_at + RET * SEQ * 4)
        w_raw = sb("w_raw", [P, RING, CHUNK])
        w_hi = sb("w_hi", [P, RING, CHUNK], F32R)
        w_lo = sb("w_lo", [P, RING, CHUNK], F32R)
        gain_post = sb("gain_post", [P, DIM])
        gain_pre = sb("gain_pre", [P, DIM])
        work = sb("work", [P, 4, SEQ])
        squares = sb("squares", [P, DIM], BF16)
        ident = sb("ident", [P, P])
        masks = sb("masks", [P, 2 * P], BF16)
        sum_post, rstd_post = sb("sum_post", [P, 16]), sb("rstd_post", [P, 16])
        sum_pre, rstd_pre = sb("sum_pre", [P, 16]), sb("rstd_pre", [P, 16])
        minus_half = sb("minus_half", [P, 4])
        gn_mean, gn_sum, gn_rstd = (sb(n, [P, 4 * RET]) for n in ("gn_mean", "gn_sum", "gn_rstd"))
        units = TILES * (MOBA + FOX)
        minus_max, row_sum, row_rec = (sb(n, [P, units]) for n in ("minus_max", "row_sum", "row_rec"))
        forget_b = sb("forget_b", [P, 1])

        ps = ctx.enter_context(nc.psum_tensor("ps", [P, 8, SEQ], F32))

        raw_landed = [sem(f"raw_landed{i}") for i in range(RING)]
        hi_done, lo_done, chunk_used = sem("hi_done"), sem("lo_done"), sem("chunk_used")
        x_landed = [sem(f"x_landed{t}") for t in range(TILES)]
        ident_landed, tables_landed = sem("ident_landed"), sem("tables_landed")
        rel_in_landed, rotary_landed = sem("rel_in_landed"), sem("rotary_landed")
        gain_pre_landed, gain_post_landed = sem("gain_pre_landed"), sem("gain_post_landed")
        select_landed = sem("select_landed")
        y_done, post_summed, post_rstd, x_updated = (
            sem(n) for n in ("y_done", "post_summed", "post_rstd", "x_updated"))
        pre_summed, pre_rstd, normed, h_turned, h_hi_done, h_ready = (
            sem(n) for n in ("pre_summed", "pre_rstd", "normed", "h_turned", "h_hi_done", "h_ready"))
        evacuated, turned_parts = sem("evacuated"), sem("turned_parts")
        gate_done, gate_scaled = sem("gate_done"), sem("gate_scaled")
        fox_v_read = sem("fox_v_read")
        rel_rows_done, rel_copied, rel_stored, rel_landed = (
            sem(n) for n in ("rel_rows_done", "rel_copied", "rel_stored", "rel_landed"))
        forget_logit, forget_log, f_ready, f_spread = (
            sem(n) for n in ("forget_logit", "forget_log", "f_ready", "f_spread"))
        ret_scored, ret_decayed, ret_out, ret_centred, ret_summed, ret_rstd, ret_normed, ret_y = (
            sem(n) for n in ("ret_scored", "ret_decayed", "ret_out", "ret_centred", "ret_summed",
                             "ret_rstd", "ret_normed", "ret_y"))
        scored, logits, exped, probs, probs_turned, probs_t_ready = (
            sem(n) for n in ("scored", "logits", "exped", "probs", "probs_turned", "probs_t_ready"))
        head_done, head_hi, head_ready = sem("head_done"), sem("head_hi"), sem("head_ready")
        silu_done, product_done, product_hi, product_ready = (
            sem(n) for n in ("silu_done", "product_done", "product_hi", "product_ready"))
        vec_step, act_step, pool_step = sem("vec_step"), sem("act_step"), sem("pool_step")
        stored = sem("stored")

        block = ctx.enter_context(nc.Block())

        def cols(t, n=1):
            return slice(t * P, (t + n) * P)

        @block.sync
        def _(sp):
            sp.dma_start(x[:, 0], x_tiles[0]).then_inc(x_landed[0], 16)
            sp.dma_start(x[:, 1], x_tiles[1]).then_inc(x_landed[1], 16)
            sp.dma_start(w_raw[:, 0], weights[0]).then_inc(raw_landed[0], 16)
            sp.dma_start(w_raw[:, 1], weights[1]).then_inc(raw_landed[1], 16)
            sp.dma_start(x[:, 2], x_tiles[2]).then_inc(x_landed[2], 16)
            sp.dma_start(w_raw[:, 2], weights[2]).then_inc(raw_landed[2], 16)
            sp.dma_start(x[:, 3], x_tiles[3]).then_inc(x_landed[3], 16)
            sp.dma_start(w_raw[:, 3], weights[3]).then_inc(raw_landed[3], 16)
            sp.dma_start(rotary[:], rotary_in).then_inc(rotary_landed, 16)
            sp.dma_start(onehot[0:BUCKETS + 1, :], onehot_in).then_inc(rel_in_landed, 16)
            sp.dma_start(rel_table[0:BUCKETS + 1, :], rel_bias).then_inc(rel_in_landed, 16)
            groups = N_CHUNKS // RING
            with nc.sync.Fori(1, groups) as g:
                for i in range(RING):
                    sp.wait_ge(lo_done, g * RING + (i + 1 - RING))
                    sp.dma_start(w_raw[:, i], weights[g * RING + i]).then_inc(raw_landed[i], 16)
            for c in range(groups * RING, N_CHUNKS):
                sp.wait_ge(lo_done, c + 1 - RING)
                sp.dma_start(w_raw[:, c % RING], weights[c]).then_inc(raw_landed[c % RING], 16)
            for t in range(TILES):
                sp.wait_ge(x_updated, 4 * 3 + t + 1)
                sp.dma_start(out_tiles[t], x[:, t]).then_inc(stored, 16)
            sp.wait_ge(stored, 16 * TILES)

        @block.gpsimd
        def _(pool):
            steps = [0]

            def low(c, group=0):
                pool.wait_ge(hi_done, group * RING + (c + 1))
                nc.gpsimd.tensor_tensor(w_lo[:, c % RING], w_raw[:, c % RING],
                                        w_hi[:, c % RING].bitcast(F32), ALU.subtract).then_inc(lo_done, 1)

            def lows(c0, c1):
                n = (c1 - c0) // RING
                if n > 1:
                    with nc.gpsimd.Fori(0, n) as g:
                        for i in range(RING):
                            low(c0 + i, g)
                    c0 += n * RING
                for c in range(c0, c1):
                    low(c)

            def own(ins):
                steps[0] += 1
                ins.then_inc(pool_step, 1)
                pool.wait_ge(pool_step, steps[0])

            def rstd(to, of, size, eps, done):
                own(nc.gpsimd.tensor_scalar(of, of, 1.0 / size, eps, ALU.mult, ALU.add))
                nc.gpsimd.tensor_tensor(to, of, minus_half[:, 0:of.shape[1]], ALU.pow).then_inc(done, 1)

            def post_rstds(b, t):
                q = 4 * (b - 1) + t
                if b:
                    pool.wait_ge(post_summed, q + 1)
                    rstd(rstd_post[:, q:q + 1], sum_post[:, q:q + 1], DIM, RMS_EPS, post_rstd)

            def pre_rstds(b, t):
                q = 4 * b + t
                if b < 4:
                    pool.wait_ge(pre_summed, q + 1)
                    rstd(rstd_pre[:, q:q + 1], sum_pre[:, q:q + 1], DIM, RMS_EPS, pre_rstd)

            def boundary(b):
                for t in range(2):
                    post_rstds(b, t)
                    pre_rstds(b, t)
                post_rstds(b, 2)
                if b < 4:
                    low(AFTER[b])
                    low(AFTER[b] + 1)
                pre_rstds(b, 2)
                post_rstds(b, 3)
                if b < 4:
                    low(AFTER[b] + 2)
                pre_rstds(b, 3)
                if b < 4:
                    low(AFTER[b] + 3)

            own(nc.gpsimd.memset(minus_half[:], -0.5))
            boundary(0)
            lows(RING, OUT0 + RING)
            pool.wait_ge(tables_landed, 16 * 4)
            for t in range(TILES):
                pool.wait_ge(gate_done, t + 1)
                nc.gpsimd.tensor_tensor(ret_gate[:, t, :], ret_gate[:, t, :], gn[:], ALU.mult).then_inc(gate_scaled, 1)
            for h in range(RET):
                pool.wait_ge(ret_summed, TILES * (h + 1))
                rstd(gn_rstd[:, 4 * h:4 * h + 4], gn_sum[:, 4 * h:4 * h + 4], HEAD, GN_EPS, ret_rstd)
                y = ret_y_rows[:, h, :].rearrange("p (t d) -> p t d", d=HEAD)
                pool.wait_ge(ret_normed, h + 1)
                nc.gpsimd.tensor_tensor(y, y, ret_gate[:, :, h * HEAD:(h + 1) * HEAD], ALU.mult).then_inc(ret_y, 1)
            at = OUT0 + RING
            for b in range(1, 4):
                lows(at, AFTER[b])
                boundary(b)
                at = AFTER[b] + RING
            lows(at, N_CHUNKS)
            boundary(4)

        @block.scalar
        def _(act):
            steps = [0]

            def own(ins):
                steps[0] += 1
                ins.then_inc(act_step, 1)
                act.wait_ge(act_step, steps[0])

            def high(c, group=0):
                if c >= RING:
                    act.wait_ge(chunk_used, group * RING + (c + 1 - RING))
                act.wait_ge(raw_landed[c % RING], group * 16 + 16 * (c // RING + 1))
                nc.scalar.activation(w_hi[:, c % RING], w_raw[:, c % RING], ACT.Copy).then_inc(hi_done, 1)

            def highs(c0, c1):
                n = (c1 - c0) // RING
                if n > 1:
                    with nc.scalar.Fori(0, n) as g:
                        for i in range(RING):
                            high(c0 + i, g)
                    c0 += n * RING
                for c in range(c0, c1):
                    high(c)

            def sum_post_squares(b, t):
                q = 4 * (b - 1) + t
                if t < 3:
                    act.wait_ge(y_done, 3 * (b - 1) + t + 1)
                else:
                    act.wait_ge(chunk_used, AFTER[b])
                if b == 4 and t:
                    act.wait_ge(post_summed, q)
                else:
                    act.wait_ge(pre_summed, 4 * b + t)
                nc.scalar.activation(squares[:], ps[:, 2 * t:2 * t + 2, :], ACT.Square,
                                     accum_out=sum_post[:, q:q + 1]).then_inc(post_summed, 1)

            def sum_pre_squares(b, t):
                q = 4 * b + t
                if b:
                    act.wait_ge(x_updated, q - 3)
                else:
                    act.wait_ge(x_landed[t], 16)
                if b:
                    act.wait_ge(post_summed, q - 3)
                elif t:
                    act.wait_ge(pre_summed, q)
                nc.scalar.activation(squares[:], x[:, t], ACT.Square,
                                     accum_out=sum_pre[:, q:q + 1]).then_inc(pre_summed, 1)

            def turned_high(b, t):
                act.wait_ge(h_turned, 4 * b + t + 1)
                nc.scalar.activation(h_hi[:, :, cols(t)],
                                     ps[:, 2 * t:2 * t + 2, :].rearrange("p a (k s) -> p (a k) s", s=P),
                                     ACT.Copy).then_inc(h_hi_done, 1)

            def boundary(b):
                def sums(t, post, pre):
                    if post and b:
                        sum_post_squares(b, t)
                    if pre and b < 4:
                        sum_pre_squares(b, t)

                sums(0, True, True)
                sums(1, True, True)
                sums(2, True, False)
                if b < 4:
                    turned_high(b, 0)
                    high(AFTER[b])
                    high(AFTER[b] + 1)
                    turned_high(b, 1)
                    high(AFTER[b] + 2)
                sums(2, False, True)
                if b < 4:
                    high(AFTER[b] + 3)
                sums(3, True, True)
                if b < 4:
                    turned_high(b, 2)
                    turned_high(b, 3)
                if b < 3:
                    act.wait_ge(normed, 4 * b + 4)
                    act.dma_start(gain_pre[:], norms[b + 1, 0].partition_broadcast(P)).then_inc(gain_pre_landed, 16)
                if 0 < b < 4:
                    act.wait_ge(x_updated, 4 * b)
                    act.dma_start(gain_post[:], norms[b, 1].partition_broadcast(P)).then_inc(gain_post_landed, 16)

            def head_high(hd):
                act.wait_ge(head_done, hd + 1)
                nc.scalar.activation(h_hi[:, hd % KT, :], ps[:, 5 + 2 * (hd % 2), :], ACT.Copy).then_inc(head_hi, 1)

            def attention(heads, unit0, head0, also={}):
                n_units = TILES * heads
                for n in range(n_units + 7):
                    if n < n_units:
                        u, i = unit0 + n, n % TILES
                        act.wait_ge(logits, u + 1)
                        nc.scalar.activation(work[:, n % 4, 0:(i + 1) * P], work[:, n % 4, 0:(i + 1) * P],
                                             ACT.Exp, bias=minus_max[:, u:u + 1], scale=-1.0,
                                             accum_out=row_sum[:, u:u + 1]).then_inc(exped, 1)
                    m = n - 3
                    if 0 <= m < n_units:
                        h, i, u = m // TILES, m % TILES, unit0 + m
                        act.wait_ge(probs_turned, u + 1)
                        if h >= 2:
                            act.wait_ge(head_done, head0 + h - 1)
                        elif unit0 == 0:
                            act.wait_ge(ret_out, RET - 1 + h)
                        nc.scalar.activation(probs_t[:, h % 2, 0:i + 1, cols(i)],
                                             ps[:, 4 + 2 * (u % 2), 0:(i + 1) * P].rearrange("p (j q) -> p j q", q=P),
                                             ACT.Copy).then_inc(probs_t_ready, 1)
                    m = n - 6
                    if m >= 0 and m % TILES == 3:
                        head_high(head0 + m // TILES)
                    if n in also:
                        also[n]()

            def ffn(c0, tile0):
                def pair(p, gate_bank, group=0, step=0):
                    at = group * step
                    high(c0 + RING + 2 * p, group if step else 0)
                    high(c0 + RING + 2 * p + 1, group if step else 0)
                    act.wait_ge(chunk_used, group * RING * bool(step) + (c0 + 2 * p + 2))
                    if tile0 + p >= 2:
                        act.wait_ge(product_done, at + (tile0 + p - 1))
                    nc.scalar.activation(work[:, p % 2, :], ps[:, gate_bank, :], ACT.Silu).then_inc(silu_done, 1)
                    act.wait_ge(product_done, at + (tile0 + p + 1))
                    nc.scalar.activation(prod_hi[:, at + p, :] if step else prod_hi[:, p, :],
                                         work[:, 2 + p % 2, :], ACT.Copy).then_inc(product_hi, 1)

                pair(0, 0)
                pair(1, 2)
                with nc.scalar.Fori(0, (FT - 2) // 2) as g:
                    pair(2, 1, g, 2)
                    pair(3, 5, g, 2)

            act.dma_start(ident[:], ident_in).then_inc(ident_landed, 16)
            act.dma_start(gain_pre[:], norms[0, 0].partition_broadcast(P)).then_inc(gain_pre_landed, 16)

            boundary(0)
            act.dma_start(gain_post[:], norms[0, 1].partition_broadcast(P)).then_inc(gain_post_landed, 16)
            act.dma_start(decay[:], decay_in).then_inc(tables_landed, 16)
            act.dma_start(gn[:], gn_gain.partition_broadcast(P)).then_inc(tables_landed, 16)
            act.dma_start(masks[:], mask_in).then_inc(tables_landed, 16)
            act.dma_start(forget_b[0:FOX, :], forget_bias).then_inc(tables_landed, 16)
            highs(QK0 + RING, QK0 + 3 * RING)
            act.wait_ge(rel_copied, 1)
            act.dma_start(bias_rows.ap(), bias_row[0:MOBA, :].unsqueeze(1).to_broadcast([MOBA, P, DIFFS])).then_inc(rel_stored, 16)
            highs(QK0 + 3 * RING, RV0 + RING)
            act.wait_ge(rel_stored, 16)
            act.dma_start(rel[:], bass.AP(bias_rows, P - 1, [[DIFFS - 1, P], [P * DIFFS, MOBA], [1, SEQ]])).then_inc(rel_landed, 16)
            highs(RV0 + RING, OUT0 + RING)
            act.wait_ge(chunk_used, OUT0)
            for t in range(TILES):
                nc.scalar.activation(ret_gate[:, t, :], ps[:, 4 + t, :], ACT.Silu).then_inc(gate_done, 1)

            def squares_of(h):
                act.wait_ge(ret_centred, h + 1)
                for t in range(TILES):
                    n = TILES * h + t
                    if n:
                        act.wait_ge(ret_summed, n)
                    nc.scalar.activation(squares[:, 0:P], ret_y_rows[:, h, cols(t)], ACT.Square,
                                         accum_out=gn_sum[:, n:n + 1]).then_inc(ret_summed, 1)

            for h in range(RET - 1):
                squares_of(h)
            attention(MOBA, 0, RET, {1: lambda: head_high(0), 2: lambda: squares_of(3), 3: lambda: head_high(1),
                                     5: lambda: head_high(2), 7: lambda: head_high(3)})
            highs(OUT0 + RING, FIN0)
            boundary(1)
            ffn(FIN0, 0)
            highs(FOUT0 + RING, QK1)
            boundary(2)
            act.dma_start(select[0:FOX, :], select_in).then_inc(select_landed, 16)
            highs(QK1 + RING, GATE1 + RING + 1)
            act.wait_ge(forget_logit, 1)
            own(nc.scalar.activation(gate_work[0:FOX, 3, :], gate_work[0:FOX, 2, :], ACT.Exp))
            nc.scalar.activation(gate_work[0:FOX, 2, :], gate_work[0:FOX, 3, :], ACT.Ln, bias=1.0).then_inc(forget_log, 1)
            highs(GATE1 + RING + 1, OUT1 + RING)
            act.wait_ge(chunk_used, OUT1)
            for t in range(TILES):
                nc.scalar.activation(fox_v[:, t, SEQ:2 * SEQ], ps[:, 4 + t, :], ACT.Copy).then_inc(fox_v_read, 1)
            attention(FOX, TILES * MOBA, KT)
            highs(OUT1 + RING, FIN1)
            boundary(3)
            ffn(FIN1, FT)
            highs(FOUT1 + RING, N_CHUNKS)
            boundary(4)

        @block.vector
        def _(vec):
            steps = [0]

            def own(ins):
                steps[0] += 1
                ins.then_inc(vec_step, 1)
                vec.wait_ge(vec_step, steps[0])

            def post(b, t):
                q = 4 * (b - 1) + t
                row = work[:, 2 * (t % 2):2 * (t % 2) + 2, :].rearrange("p a s -> p (a s)")
                vec.wait_ge(gain_post_landed, 16 * b)
                vec.wait_ge(post_rstd, q + 1)
                if t >= 2:
                    vec.wait_ge(x_updated, q - 1)
                    if b < 4:
                        vec.wait_ge(h_turned, 4 * b + t - 1)
                own(nc.vector.scalar_tensor_tensor(
                    out=row, in0=ps[:, 2 * t:2 * t + 2, :].rearrange("p a s -> p (a s)"),
                    scalar=rstd_post[:, q:q + 1], in1=gain_post[:], op0=ALU.mult, op1=ALU.mult))
                nc.vector.tensor_tensor(x[:, t], x[:, t], row, ALU.add).then_inc(x_updated, 1)

            def pre(b, t):
                q = 4 * b + t
                row = work[:, 2 * (t % 2):2 * (t % 2) + 2, :].rearrange("p a s -> p (a s)")
                vec.wait_ge(gain_pre_landed, 16 * (b + 1))
                vec.wait_ge(pre_rstd, q + 1)
                if b:
                    vec.wait_ge(x_updated, q - 3)
                elif t >= 2:
                    vec.wait_ge(h_turned, q - 1)
                nc.vector.scalar_tensor_tensor(
                    out=row, in0=x[:, t], scalar=rstd_pre[:, q:q + 1], in1=gain_pre[:],
                    op0=ALU.mult, op1=ALU.mult).then_inc(normed, 1)

            def turned_low(b, t):
                vec.wait_ge(h_hi_done, 4 * b + t + 1)
                nc.vector.tensor_tensor(
                    h_lo[:, :, cols(t)], ps[:, 2 * t:2 * t + 2, :].rearrange("p a (k s) -> p (a k) s", s=P),
                    h_hi[:, :, cols(t)].bitcast(F32), ALU.subtract).then_inc(h_ready, 1)

            def boundary(b):
                if b in (2, 4):
                    vec.wait_ge(product_ready, FT * b // 2)
                if b:
                    post(b, 0)
                if b < 4:
                    pre(b, 0)
                if b:
                    post(b, 1)
                if b < 4:
                    pre(b, 1)
                    turned_low(b, 0)
                if b:
                    post(b, 2)
                if b < 4:
                    turned_low(b, 1)
                    pre(b, 2)
                if b:
                    post(b, 3)
                if b < 4:
                    pre(b, 3)
                    turned_low(b, 2)
                    turned_low(b, 3)

            def evacuate(to, bank, scale=None):
                if scale is None:
                    ins = nc.vector.tensor_copy(to, ps[:, bank, :])
                else:
                    ins = nc.vector.tensor_scalar(to, ps[:, bank, :], scale, None, ALU.mult)
                ins.then_inc(evacuated, 1)

            def head_low(hd):
                vec.wait_ge(head_hi, hd + 1)
                nc.vector.tensor_tensor(h_lo[:, hd % KT, :], ps[:, 5 + 2 * (hd % 2), :],
                                        h_hi[:, hd % KT, :].bitcast(F32), ALU.subtract).then_inc(head_ready, 1)

            def attention(heads, unit0, head0, table, also={}):
                n_units = TILES * heads
                for n in range(n_units + 8):
                    if n < n_units:
                        u, h, i = unit0 + n, n // TILES, n % TILES
                        vec.wait_ge(scored, u + 1)
                        if n >= 4:
                            vec.wait_ge(probs_turned, u - 3)
                        nc.vector.tensor_tensor_reduce(
                            work[:, n % 4, 0:(i + 1) * P], ps[:, u % 4, 0:(i + 1) * P], table(h, i),
                            -1.0, float(np.finfo(np.float32).max), ALU.add, ALU.min,
                            minus_max[:, u:u + 1]).then_inc(logits, 1)
                    m = n - 1
                    if 0 <= m < n_units:
                        u, i = unit0 + m, m % TILES
                        vec.wait_ge(exped, u + 1)
                        own(nc.vector.reciprocal(row_rec[:, u:u + 1], row_sum[:, u:u + 1]))
                        nc.vector.tensor_scalar(work[:, m % 4, 0:(i + 1) * P], work[:, m % 4, 0:(i + 1) * P],
                                                row_rec[:, u:u + 1], None, ALU.mult).then_inc(probs, 1)
                    m = n - 7
                    if m >= 0 and m % TILES == 3:
                        head_low(head0 + m // TILES)
                    if n in also:
                        also[n]()

            def ffn(c0, tile0):
                def pair(p, up_bank, group=0, step=0):
                    at = group * step
                    vec.wait_ge(silu_done, at + (tile0 + p + 1))
                    if tile0 + p >= 2:
                        vec.wait_ge(product_ready, at + (tile0 + p - 1))
                    nc.vector.tensor_tensor(work[:, 2 + p % 2, :], work[:, p % 2, :], ps[:, up_bank, :],
                                            ALU.mult).then_inc(product_done, 1)
                    vec.wait_ge(product_hi, at + (tile0 + p + 1))
                    tile = at + p if step else p
                    nc.vector.tensor_tensor(prod_lo[:, tile, :], work[:, 2 + p % 2, :],
                                            prod_hi[:, tile, :].bitcast(F32), ALU.subtract).then_inc(product_ready, 1)

                pair(0, 1)
                pair(1, 3)
                with nc.vector.Fori(0, (FT - 2) // 2) as g:
                    pair(2, 3, g, 2)
                    pair(3, 7, g, 2)

            boundary(0)
            vec.wait_ge(rotary_landed, 16)
            for i in range(2 * RET):
                vec.wait_ge(chunk_used, QK0 + i + 1)
                to, bank = ret_qk[:, i, :], ps[:, i % 4, :]
                nc.vector.tensor_tensor(to, bank, rotary[:, 0, :], ALU.mult).then_inc(turned_parts, 1)
                if i:
                    vec.wait_ge(evacuated, i)
                nc.vector.tensor_tensor(turned[0:64, :], ps[64:128, i % 4, :], rotary[64:128, 1, :],
                                        ALU.mult).then_inc(turned_parts, 1)
                nc.vector.tensor_tensor(turned[64:128, :], ps[0:64, i % 4, :], rotary[0:64, 1, :],
                                        ALU.mult).then_inc(turned_parts, 1)
                vec.wait_ge(turned_parts, 3 * (i + 1))
                nc.vector.tensor_tensor(to, to, turned[:], ALU.add).then_inc(evacuated, 1)
                if i == RING:
                    vec.wait_ge(rel_rows_done, 2)
                    nc.vector.tensor_copy(bias_row[0:MOBA, :].rearrange("h (a s) -> h a s", a=2),
                                          ps[0:MOBA, 6:8, 0:DIFFS // 2]).then_inc(rel_copied, 1)
            for i in range(2 * MOBA):
                vec.wait_ge(chunk_used, QK0 + 2 * RET + i + 1)
                evacuate(moba_qk[:, i, :], i % 4, SCALE if i < MOBA else None)
            vec.wait_ge(chunk_used, MV0)
            for t in range(TILES):
                evacuate(ret_v[:, t, :], 4 + t)
            vec.wait_ge(chunk_used, RG0)
            for t in range(TILES):
                evacuate(moba_v[:, t, :], t)
            vec.wait_ge(tables_landed, 16 * 4)
            vec.wait_ge(rel_landed, 16)

            def decays(h):
                for j in range(TILES):
                    vec.wait_ge(ret_scored, 4 * h + j + 1)
                    if h >= 2:
                        vec.wait_ge(ret_out, h - 1)
                    nc.vector.tensor_tensor(probs_t[:, h % 2, j, 0:SEQ - j * P], ps[:, j, 0:SEQ - j * P],
                                            decay[:, h, 0:SEQ - j * P], ALU.mult).then_inc(ret_decayed, 1)

            def by_tile(row):
                return row.rearrange("p (t d) -> p t d", d=HEAD)

            def centre(h):
                bank, mean = by_tile(ps[:, 4 + 2 * (h % 2), :]), gn_mean[:, 4 * h:4 * h + 4]
                vec.wait_ge(ret_out, h + 1)
                own(nc.vector.tensor_reduce(mean, bank, AX_X, ALU.add))
                own(nc.vector.tensor_scalar(mean, mean, 1.0 / HEAD, None, ALU.mult))
                nc.vector.tensor_tensor(by_tile(ret_y_rows[:, h, :]), bank, mean.unsqueeze(2).to_broadcast([P, TILES, HEAD]),
                                        ALU.subtract).then_inc(ret_centred, 1)

            def norm(h):
                y = by_tile(ret_y_rows[:, h, :])
                vec.wait_ge(ret_rstd, h + 1)
                vec.wait_ge(ret_centred, h + 1)
                nc.vector.tensor_tensor(
                    y, y, gn_rstd[:, 4 * h:4 * h + 4].unsqueeze(2).to_broadcast([P, TILES, HEAD]),
                    ALU.mult).then_inc(ret_normed, 1)

            for h in range(RET):
                decays(h)
                if h:
                    centre(h - 1)
                if h >= 2:
                    norm(h - 2)
            attention(MOBA, 0, RET, lambda h, i: rel[:, h, (TILES - 1 - i) * P:SEQ],
                      {0: lambda: norm(2), 1: lambda: centre(3), 2: lambda: head_low(0),
                       3: lambda: head_low(1), 4: lambda: norm(3), 6: lambda: head_low(2), 7: lambda: head_low(3)})
            boundary(1)
            ffn(FIN0, 0)
            boundary(2)
            first = 2 * (RET + MOBA) + 2 * TILES
            for scale, g0 in ((SCALE, 0), (None, FOX // 4)):
                with nc.vector.Fori(g0, g0 + FOX // 4) as g:
                    for i in range(4):
                        vec.wait_ge(chunk_used, g * 4 + (QK1 + i + 1))
                        evacuate(fox_qk[:, g * 4 + i, :], i, scale)
            z, low, neg, one, total = (gate_work[0:FOX, n, :] for n in range(5))
            vec.wait_ge(chunk_used, GATE1 + 1)
            own(nc.vector.tensor_scalar(z, ps[0:FOX, 4, :], forget_b[0:FOX, :], None, ALU.add))
            own(nc.vector.tensor_scalar(low, z, 0.0, None, ALU.min))
            nc.vector.scalar_tensor_tensor(out=neg, in0=low, scalar=2.0, in1=z, op0=ALU.mult,
                                           op1=ALU.subtract).then_inc(forget_logit, 1)
            vec.wait_ge(forget_log, 1)
            own(nc.vector.tensor_tensor(z, low, neg, ALU.subtract))
            own(nc.vector.memset(one, 1.0))
            nc.vector.tensor_tensor_scan(total, one, z, 0.0, ALU.mult, ALU.add).then_inc(f_ready, 1)
            vec.wait_ge(chunk_used, V1 + 4)
            for t in range(TILES):
                evacuate(fox_v[:, t, 0:SEQ], t)
            for h in range(FOX):
                vec.wait_ge(f_spread, h + 1)
                evacuate(minus_f[:, h, :], h % TILES)
            attention(FOX, TILES * MOBA, KT, lambda h, i: minus_f[:, h, 0:(i + 1) * P])
            boundary(3)
            ffn(FIN1, FT)
            boundary(4)

        @block.tensor
        def _(pe):
            mm = nc.tensor.matmul

            def exact(to, held, moved, start, stop):
                mm(to, held[0], moved[0], start=start, stop=False)
                mm(to, held[0], moved[1], start=False, stop=False)
                return mm(to, held[1], moved[0], start=False, stop=stop)

            def column_chunk(c, bank, at=slice(0, SEQ)):
                for k in range(KT):
                    last = exact(ps[:, bank, at], [w[:, c % RING, cols(k)] for w in (w_hi, w_lo)],
                                 [h[:, k, at] for h in (h_hi, h_lo)], k == 0, k == KT - 1)
                return last

            def row_chunk(c, k0, n_k, banks, tiles=range(TILES), source=(h_hi, h_lo)):
                for kk in range(2):
                    k = k0 + kk
                    for t in tiles:
                        last = exact(ps[:, banks[t], :], [s[:, k, cols(t)] for s in source],
                                     [w[:, c % RING, kk * SEQ:(kk + 1) * SEQ] for w in (w_hi, w_lo)],
                                     k == 0, k == n_k - 1)
                return last

            def turn(b, t):
                pe.wait_ge(normed, 4 * b + t + 1)
                for k in range(KT):
                    last = nc.tensor.transpose(ps[:, 2 * t + k // 4, cols(k % 4)],
                                               work[:, 2 * (t % 2) + k // 4, cols(k % 4)], ident[:])
                last.then_inc(h_turned, 1)

            def first_columns(b):
                c0 = AFTER[b]
                pe.wait_ge(h_ready, 4 * b + 2)
                for i in range(RING):
                    if i == RING - 1:
                        turn(b, 2)
                        turn(b, 3)
                    pe.wait_ge(lo_done, c0 + i + 1)
                    column_chunk(c0 + i, i, slice(0, SEQ // 2))
                pe.wait_ge(h_ready, 4 * b + 4)
                for i in range(RING):
                    column_chunk(c0 + i, i, slice(SEQ // 2, SEQ)).then_inc(chunk_used, 1)

            def rows(c0, n, n_k, banks, source=(h_hi, h_lo), ready=None, k0=0):
                for i in range(n):
                    if ready is not None:
                        ready(k0 + 2 * i + 1)
                    pe.wait_ge(lo_done, c0 + i + 1)
                    row_chunk(c0 + i, k0 + 2 * i, n_k, banks, source=source).then_inc(chunk_used, 1)

            def last_rows(b, k0, n_k, banks, source=(h_hi, h_lo)):
                c0 = AFTER[b] - RING
                for t in range(TILES):
                    for i in range(RING):
                        if t == 0:
                            pe.wait_ge(lo_done, c0 + i + 1)
                        if b < 4 and t == TILES - 1 and i in (0, 2):
                            turn(b, i // 2)
                        last = row_chunk(c0 + i, k0 + 2 * i, n_k, banks, (t,), source)
                        if t == TILES - 1:
                            last.then_inc(chunk_used, 1)
                        elif i == RING - 1:
                            last.then_inc(y_done, 1)

            halves = [[2 * t + half for t in range(TILES)] for half in range(2)]

            def project_out(b, c0, head0):
                def ready(k):
                    pe.wait_ge(head_ready, head0 + k + 1)
                rows(c0, 4, KT, halves[0], ready=ready)
                last_rows(b, 0, KT, halves[1])

            def ffn(b, c_in, c_out, tile0):
                first_columns(b)
                with nc.tensor.Fori(0, (2 * FT - RING) // RING) as g:
                    for i in range(RING):
                        p = (RING + i) // 2
                        pe.wait_ge(product_done, g * 2 + (tile0 + p - 1 + i % 2))
                        pe.wait_ge(lo_done, g * RING + (c_in + RING + i + 1))
                        column_chunk((c_in + i) % RING, 2 * i + 1).then_inc(chunk_used, 1)

                def ready(k):
                    pe.wait_ge(product_ready, tile0 + k + 1)
                source = (prod_hi, prod_lo)
                rows(c_out, FT // 2, FT, halves[0], source, ready)
                rows(c_out + FT // 2, FT // 2 - RING, FT, halves[1], source)
                last_rows(b + 1, FT - 2 * RING, FT, halves[1], source)

            def attention(heads, unit0, head0, q, k, v, masked, also={}):
                n_units = TILES * heads
                for n in range(n_units + 6):
                    if n < n_units:
                        u, h, i = unit0 + n, n // TILES, n % TILES
                        if n >= 4:
                            pe.wait_ge(logits, u - 3)
                        elif masked:
                            pe.wait_ge(evacuated, first + 2 * FOX + TILES + TILES + n + 1)
                        else:
                            pe.wait_ge(ret_decayed, 4 * (RET - 1) + n + 1)
                        last = mm(ps[:, u % 4, 0:(i + 1) * P], q[:, h, cols(i)], k[:, h, 0:(i + 1) * P],
                                  start=True, stop=True)
                        if masked:
                            last = mm(ps[:, u % 4, cols(i)], masks[:, 0:P], masks[:, P:2 * P],
                                      start=False, stop=True, skip_group_check=True)
                        last.then_inc(scored, 1)
                    m = n - 3
                    if 0 <= m < n_units:
                        u, i = unit0 + m, m % TILES
                        pe.wait_ge(probs, u + 1)
                        if u >= 2:
                            pe.wait_ge(probs_t_ready, u - 1)
                        else:
                            pe.wait_ge(ret_centred, RET - 1 + u)
                        for j in range(i + 1):
                            last = nc.tensor.transpose(ps[:, 4 + 2 * (u % 2), cols(j)],
                                                       work[:, m % 4, cols(j)], ident[:])
                        last.then_inc(probs_turned, 1)
                    m = n - 5
                    if m >= 0 and m % TILES == 3:
                        h, hd = m // TILES, head0 + m // TILES
                        pe.wait_ge(probs_t_ready, unit0 + m + 1)
                        if hd >= 2:
                            pe.wait_ge(head_ready, hd - 1)
                        for j in range(TILES):
                            last = mm(ps[:, 5 + 2 * (hd % 2), j * P:SEQ], v[:, j, h * HEAD:(h + 1) * HEAD],
                                      probs_t[:, h % 2, j, j * P:SEQ], start=j == 0, stop=j == TILES - 1)
                        last.then_inc(head_done, 1)
                    if n in also:
                        also[n]()

            pe.wait_ge(ident_landed, 16)
            turn(0, 0)
            turn(0, 1)
            first_columns(0)
            pe.wait_ge(rel_in_landed, 32)
            for half in range(2):
                mm(ps[0:MOBA, 6 + half, 0:DIFFS // 2], rel_table[0:BUCKETS + 1, :],
                   onehot[0:BUCKETS + 1, half * (DIFFS // 2):(half + 1) * (DIFFS // 2)],
                   start=True, stop=True).then_inc(rel_rows_done, 1)
            with nc.tensor.Fori(1, (RV0 - QK0) // RING) as g:
                for i in range(RING):
                    pe.wait_ge(evacuated, g * RING + (i + 1 - RING))
                    pe.wait_ge(lo_done, g * RING + (QK0 + i + 1))
                    column_chunk(i, i).then_inc(chunk_used, 1)
            pe.wait_ge(rel_copied, 1)
            rows(RV0, 4, KT, [4, 5, 6, 7])
            pe.wait_ge(evacuated, RV0)
            rows(MV0, 4, KT, [0, 1, 2, 3])
            pe.wait_ge(evacuated, RV0 + TILES)
            rows(RG0, 4, KT, [4, 5, 6, 7])
            pe.wait_ge(evacuated, RV0 + 2 * TILES)

            def ret_scores(h):
                for j in range(TILES):
                    if h >= 1:
                        pe.wait_ge(ret_decayed, 4 * (h - 1) + j + 1)
                    mm(ps[:, j, 0:SEQ - j * P], ret_qk[:, RET + h, cols(j)], ret_qk[:, h, j * P:SEQ],
                       start=True, stop=True).then_inc(ret_scored, 1)

            def ret_output(h):
                pe.wait_ge(ret_decayed, 4 * h + 4)
                if h >= 2:
                    pe.wait_ge(ret_centred, h - 1)
                for i in range(TILES):
                    for j in range(i + 1):
                        last = mm(ps[:, 4 + 2 * (h % 2), cols(i)], probs_t[:, h % 2, j, cols(i - j)],
                                  ret_v[:, j, h * HEAD:(h + 1) * HEAD], start=j == 0, stop=j == i)
                last.then_inc(ret_out, 1)

            def ret_turn(h):
                pe.wait_ge(ret_y, h + 1)
                if h >= 2:
                    pe.wait_ge(head_ready, h - 1)
                for t in range(TILES):
                    last = nc.tensor.transpose(ps[:, 5 + 2 * (h % 2), cols(t)], ret_y_rows[:, h, cols(t)], ident[:])
                last.then_inc(head_done, 1)

            ret_scores(0)
            ret_scores(1)
            pe.wait_ge(gate_done, TILES)
            ret_output(0)
            ret_scores(2)
            ret_output(1)
            ret_scores(3)
            ret_output(2)

            def last_output():
                ret_turn(0)
                ret_output(3)

            attention(MOBA, 0, RET, moba_qk[:, 0:MOBA], moba_qk[:, MOBA:2 * MOBA], moba_v, False,
                      {1: last_output, 2: lambda: ret_turn(1), 4: lambda: ret_turn(2), 6: lambda: ret_turn(3)})
            project_out(1, OUT0, 0)
            ffn(1, FIN0, FOUT0, 0)
            first = 2 * (RET + MOBA) + 2 * TILES
            first_columns(2)
            with nc.tensor.Fori(1, 2 * FOX // RING) as g:
                for i in range(RING):
                    pe.wait_ge(evacuated, g * RING + (first + i + 1 - RING))
                    pe.wait_ge(lo_done, g * RING + (QK1 + i + 1))
                    column_chunk((QK1 + i) % RING, i).then_inc(chunk_used, 1)
            pe.wait_ge(lo_done, GATE1 + 1)
            column_chunk(GATE1, 4).then_inc(chunk_used, 1)
            pe.wait_ge(evacuated, first + 2 * FOX)
            rows(V1, 4, KT, [0, 1, 2, 3])
            pe.wait_ge(f_ready, 1)
            pe.wait_ge(select_landed, 16)
            for i in range(4):
                rows(V1 + 4 + i, 1, KT, [4, 5, 6, 7], k0=2 * i)
                for h in (2 * i, 2 * i + 1):
                    pe.wait_ge(evacuated, first + 2 * FOX + h + 1)
                    mm(ps[:, h % TILES, :], select[0:FOX, cols(h)], gate_work[0:FOX, 4, :],
                       start=True, stop=True).then_inc(f_spread, 1)
            pe.wait_ge(fox_v_read, TILES)
            attention(FOX, TILES * MOBA, KT, fox_qk[:, 0:FOX], fox_qk[:, FOX:2 * FOX], fox_v, True)
            project_out(3, OUT1, KT)
            ffn(3, FIN1, FOUT1, FT)


def constants():
    f32 = np.float32
    ident = np.eye(P, dtype=f32)
    mask = np.where(np.arange(P)[None, :] > np.arange(P)[:, None], NEG, 0.0)
    gap = np.arange(SEQ)[None, :] - np.arange(P)[:, None]
    log_g = np.log1p(-(2.0 ** (-5.0 - np.arange(RET))))
    decay = np.where(gap[:, None, :] >= 0, np.exp(log_g[None, :, None] * np.maximum(gap, 0)[:, None, :]), 0.0)
    inv = np.power(f32(10000.0), -np.arange(0, HEAD, 2, dtype=f32) / f32(HEAD)).astype(f32)
    angle = (np.arange(SEQ, dtype=f32)[None, :] * inv[:, None]).astype(f32).astype(np.float64)
    cos, sin = np.cos(angle), np.sin(angle)
    rotary = np.stack([np.concatenate([cos, cos]), np.concatenate([sin, -sin])], axis=1)
    rel = SEQ - 1 - np.arange(DIFFS)
    n = np.maximum(rel, 0)
    exact = BUCKETS // 2
    large = exact + (np.log(np.maximum(n, 1).astype(f32) / exact) / np.log(128 / exact)
                     * (BUCKETS - exact)).astype(np.int32)
    bucket = np.where(n < exact, n, np.minimum(large, BUCKETS - 1))
    onehot = np.zeros((BUCKETS + 1, DIFFS), f32)
    onehot[bucket, np.arange(DIFFS)] = rel >= 0
    onehot[BUCKETS] = np.where(rel < 0, NEG, 0.0)
    select = -np.repeat(np.eye(FOX, dtype=f32), P, axis=1)
    return ident, mask, (decay * SCALE).astype(f32), rotary.astype(f32), onehot, select


def column_chunks(w):
    n = w.shape[1] // P
    return w.reshape(KT, P, n, P).transpose(2, 1, 0, 3).reshape(n, P, KT * P)


def row_chunks(w):
    k, n = w.shape[0] // (2 * P), w.shape[1] // SEQ
    return w.reshape(k, 2, P, n, SEQ).transpose(3, 0, 2, 1, 4).reshape(n * k, P, 2 * SEQ)


def ffn_chunks(w_in, w_out):
    both = np.stack([column_chunks(w_in[:, :HIDDEN]), column_chunks(w_in[:, HIDDEN:])], axis=1)
    return [both.reshape(2 * FT, P, CHUNK), row_chunks(w_out)]


def kernel(x, rel_bias, norm_mix_pre, norm_mix_post, norm_ffn_pre, norm_ffn_post, even_w_in, even_gn,
           even_w_out, odd_w_in, odd_b_forget, odd_w_out, ffn_w_in, ffn_w_out):
    import concourse.bacc as bacc
    from concourse.bass_utils import run_bass_kernel_spmd
    import ml_dtypes

    a = np.asarray
    even, odd = a(even_w_in)[0], a(odd_w_in)[0]
    ffn_in, ffn_out = a(ffn_w_in), a(ffn_w_out)
    rw, mw, fw = RET * HEAD, MOBA * HEAD, FOX * HEAD
    q_and_k = np.concatenate([even[:, :2 * rw], even[:, 4 * rw:4 * rw + 2 * mw]], axis=1)
    gate = np.concatenate([odd[:, 3 * fw:], np.zeros((DIM, P - FOX), np.float32)], axis=1)
    stream = np.concatenate([
        column_chunks(q_and_k), row_chunks(even[:, 2 * rw:3 * rw]), row_chunks(even[:, 4 * rw + 2 * mw:]),
        row_chunks(even[:, 3 * rw:4 * rw]), row_chunks(a(even_w_out)[0]),
        *ffn_chunks(ffn_in[0], ffn_out[0]),
        column_chunks(odd[:, :2 * fw]), column_chunks(gate), row_chunks(odd[:, 2 * fw:3 * fw]),
        row_chunks(a(odd_w_out)[0]),
        *ffn_chunks(ffn_in[1], ffn_out[1]),
    ])
    assert stream.shape == (N_CHUNKS, P, CHUNK)
    pre = [a(norm_mix_pre)[0], a(norm_ffn_pre)[0], a(norm_mix_pre)[1], a(norm_ffn_pre)[1]]
    post = [a(norm_mix_post)[0], a(norm_ffn_post)[0], a(norm_mix_post)[1], a(norm_ffn_post)[1]]
    ident, mask, decay, rotary, onehot, select = constants()
    arrays = {
        "x_in": a(x)[0],
        "weights": stream,
        "norms": np.stack([np.stack(pre), np.stack(post)], axis=1),
        "gn_gain": a(even_gn)[0],
        "rel_bias": np.concatenate([a(rel_bias), np.ones((1, MOBA), np.float32)]),
        "forget_bias": a(odd_b_forget)[0][:, None],
        "ident_in": ident,
        "mask_in": np.concatenate([ident, mask], axis=1).astype(ml_dtypes.bfloat16),
        "decay_in": decay,
        "rotary_in": rotary,
        "onehot_in": onehot,
        "select_in": select,
    }
    nc = bacc.Bacc("TRN2", target_bir_lowering=False, num_devices=1)
    arrays = {n: np.ascontiguousarray(v) for n, v in arrays.items()}
    args = {n: nc.dram_tensor(n, v.shape, mybir.dt.from_np(v.dtype), kind="ExternalInput").ap()
            for n, v in arrays.items()}
    out = nc.dram_tensor("out", (SEQ, DIM), F32, kind="ExternalOutput").ap()
    build(nc, **args, out=out)
    result = run_bass_kernel_spmd(nc, [arrays], core_ids=[0])
    return result.results[0]["out"].reshape(1, SEQ, DIM)
```

```python
from contextlib import ExitStack

import numpy as np

import concourse.bass as bass
from concourse import mybir

F32 = mybir.dt.float32
F32R = mybir.dt.float32r
BF16 = mybir.dt.bfloat16
ALU = mybir.AluOpType
ACT = mybir.ActivationFunctionType
AX_X = mybir.AxisListType.X

P = 128
SEQ, DIM, HEAD = 512, 1024, 128
TILES = SEQ // P
KT = DIM // P
RET, MOBA, FOX = 4, 4, 8
HIDDEN = 2816
FT = HIDDEN // P
BUCKETS = 32
MOBA_BLOCK, MOBA_TOPK = 256, 3
assert SEQ // MOBA_BLOCK <= MOBA_TOPK
NEG = -1e30
RMS_EPS, GN_EPS = 1e-6, 1e-5
SCALE = HEAD ** -0.5
DIFFS = SEQ + P

QUERY_ORDER = (3, 0, 2, 1)

RING = 4
CHUNK = 1024
QK0 = 0
RV0 = QK0 + 2 * (RET + MOBA)
RG0 = RV0 + 4
MV0 = RG0 + 4
OUT0 = MV0 + 4
FIN0 = OUT0 + 8
FOUT0 = FIN0 + 2 * FT
QK1 = FOUT0 + FT
GATE1 = QK1 + 2 * FOX
V1 = GATE1 + 1
OUT1 = V1 + 8
FIN1 = OUT1 + 8
FOUT1 = FIN1 + 2 * FT
N_CHUNKS = FOUT1 + FT
AFTER = [QK0, FIN0, QK1, FIN1, N_CHUNKS]


def build(nc, x_in, weights, norms, gn_gain, rel_bias, forget_bias, ident_in, mask_in, decay_in,
          rotary_in, onehot_in, select_in, out):
    x_tiles = x_in.rearrange("(t p) d -> t p d", p=P)
    out_tiles = out.rearrange("(t p) d -> t p d", p=P)
    bias_rows = nc.dram_tensor("bias_rows", [MOBA, P, DIFFS], F32, kind="Internal")

    with ExitStack() as ctx:
        def sb(name, shape, dt=F32):
            return ctx.enter_context(nc.sbuf_tensor(name, shape, dt))

        def sem(name):
            return ctx.enter_context(nc.semaphore(name))

        arena_at = (nc.sbuf_base + 31) // 32 * 32
        sb("arena", [P, 90 * 256 + 8])

        def arena(name, shape, kib, dt=F32):
            return nc.alloc_sbuf_tensor_at(name, shape, dt, offset=arena_at + kib * 1024)

        ret_qk = arena("ret_qk", [P, 2 * RET, SEQ], 0)
        moba_qk = arena("moba_qk", [P, 2 * MOBA, SEQ], 16)
        ret_v = arena("ret_v", [P, TILES, RET * HEAD], 32)
        moba_v = arena("moba_v", [P, TILES, MOBA * HEAD], 40)
        ret_gate = arena("ret_gate", [P, TILES, RET * HEAD], 48)
        decay = arena("decay", [P, RET, SEQ], 56)
        rel = arena("rel", [P, MOBA, SEQ], 64)
        gn = arena("gn", [P, RET * HEAD], 72)
        probs_t = arena("probs_t", [P, 2, TILES, SEQ], 74)
        rotary = arena("rotary", [P, 2, SEQ], 74)
        turned = arena("turned", [P, SEQ], 78)
        onehot = arena("onehot", [P, DIFFS], 80)
        bias_row = arena("bias_row", [P, DIFFS], 83)
        rel_table = arena("rel_table", [P, MOBA], 86)
        fox_qk = arena("fox_qk", [P, 2 * FOX, SEQ], 0)
        fox_v = arena("fox_v", [P, TILES, FOX * HEAD], 32)
        minus_f = arena("minus_f", [P, FOX, SEQ], 48)
        select = arena("select", [P, FOX * P], 64)
        select_r = arena("select_r", [P, FOX * P], 68, F32R)
        f_hi = arena("f_hi", [P, SEQ], 72, F32R)
        f_lo = arena("f_lo", [P, SEQ], 74, F32R)
        gate_work = arena("gate_work", [P, 5, SEQ], 78)
        prod_hi = arena("prod_hi", [P, FT, SEQ], 0, F32R)
        prod_lo = arena("prod_lo", [P, FT, SEQ], 44, F32R)

        x = sb("x", [P, TILES, DIM])
        h_hi = sb("h_hi", [P, KT, SEQ], F32R)
        h_lo = sb("h_lo", [P, KT, SEQ], F32R)
        w_raw = sb("w_raw", [P, RING, CHUNK])
        w_hi = sb("w_hi", [P, RING, CHUNK], F32R)
        w_lo = sb("w_lo", [P, RING, CHUNK], F32R)
        gains_at = (nc.sbuf_base + 31) // 32 * 32
        gain_post = sb("gain_post", [P, DIM])
        gain_pre = sb("gain_pre", [P, DIM])
        ret_y_rows = nc.alloc_sbuf_tensor_at("ret_y_rows", [P, RET, SEQ], F32, offset=gains_at)
        work = sb("work", [P, 4, SEQ])
        squares = sb("squares", [P, DIM], BF16)
        ident = sb("ident", [P, P])
        masks = sb("masks", [P, 2 * P], BF16)
        sum_post, rstd_post = sb("sum_post", [P, 16]), sb("rstd_post", [P, 16])
        sum_pre, rstd_pre = sb("sum_pre", [P, 16]), sb("rstd_pre", [P, 16])
        minus_half, last_sum = sb("minus_half", [P, 4]), sb("last_sum", [P, 2])
        gn_mean, gn_sum, gn_rstd = (sb(n, [P, 4 * RET]) for n in ("gn_mean", "gn_sum", "gn_rstd"))
        units = TILES * (MOBA + FOX)
        minus_max, row_sum, row_rec = (sb(n, [P, units]) for n in ("minus_max", "row_sum", "row_rec"))
        forget_b = sb("forget_b", [P, 1])

        ps = ctx.enter_context(nc.psum_tensor("ps", [P, 8, SEQ], F32))

        raw_landed = [sem(f"raw_landed{i}") for i in range(RING)]
        hi_done, lo_done, chunk_used = sem("hi_done"), sem("lo_done"), sem("chunk_used")
        x_landed = [sem(f"x_landed{t}") for t in range(TILES)]
        ident_landed, tables_landed = sem("ident_landed"), sem("tables_landed")
        rel_in_landed, rotary_landed = sem("rel_in_landed"), sem("rotary_landed")
        gain_pre_landed, gain_post_landed = sem("gain_pre_landed"), sem("gain_post_landed")
        select_landed, select_ready = sem("select_landed"), sem("select_ready")
        y_done, post_summed, post_rstd, x_updated = (
            sem(n) for n in ("y_done", "post_summed", "post_rstd", "x_updated"))
        pre_summed, pre_rstd, normed, h_turned, h_hi_done, h_ready = (
            sem(n) for n in ("pre_summed", "pre_rstd", "normed", "h_turned", "h_hi_done", "h_ready"))
        evacuated, turned_parts = sem("evacuated"), sem("turned_parts")
        gate_done, gate_scaled = sem("gate_done"), sem("gate_scaled")
        moba_v_done, moba_v_read = sem("moba_v_done"), sem("moba_v_read")
        v_done, fox_v_read = sem("v_done"), sem("fox_v_read")
        rel_rows_done, rel_copied, rel_stored, rel_landed = (
            sem(n) for n in ("rel_rows_done", "rel_copied", "rel_stored", "rel_landed"))
        forget_logit, forget_log, f_ready, f_spread = (
            sem(n) for n in ("forget_logit", "forget_log", "f_ready", "f_spread"))
        ret_scored, ret_decayed, ret_out, ret_centred, ret_summed, ret_rstd, ret_normed, ret_y = (
            sem(n) for n in ("ret_scored", "ret_decayed", "ret_out", "ret_centred", "ret_summed",
                             "ret_rstd", "ret_normed", "ret_y"))
        scored, logits, exped, probs, probs_turned, probs_t_ready = (
            sem(n) for n in ("scored", "logits", "exped", "probs", "probs_turned", "probs_t_ready"))
        head_done, head_hi, head_ready = sem("head_done"), sem("head_hi"), sem("head_ready")
        silu_done, product_done, product_hi, product_ready = (
            sem(n) for n in ("silu_done", "product_done", "product_hi", "product_ready"))
        vec_step, act_step, pool_step = sem("vec_step"), sem("act_step"), sem("pool_step")
        last_summed = sem("last_summed")
        stored = sem("stored")

        block = ctx.enter_context(nc.Block())

        def cols(t, n=1):
            return slice(t * P, (t + n) * P)

        @block.sync
        def _(sp):
            sp.dma_start(x[:, 0], x_tiles[0]).then_inc(x_landed[0], 16)
            sp.dma_start(x[:, 1], x_tiles[1]).then_inc(x_landed[1], 16)
            sp.dma_start(onehot[0:BUCKETS + 1, :], onehot_in).then_inc(rel_in_landed, 16)
            sp.dma_start(rel_table[0:BUCKETS + 1, :], rel_bias).then_inc(rel_in_landed, 16)
            sp.dma_start(w_raw[:, 0], weights[0]).then_inc(raw_landed[0], 16)
            sp.dma_start(w_raw[:, 1], weights[1]).then_inc(raw_landed[1], 16)
            sp.dma_start(x[:, 2], x_tiles[2]).then_inc(x_landed[2], 16)
            sp.dma_start(w_raw[:, 2], weights[2]).then_inc(raw_landed[2], 16)
            sp.dma_start(x[:, 3], x_tiles[3]).then_inc(x_landed[3], 16)
            sp.dma_start(w_raw[:, 3], weights[3]).then_inc(raw_landed[3], 16)
            sp.dma_start(rotary[:], rotary_in).then_inc(rotary_landed, 16)
            groups = N_CHUNKS // RING
            with nc.sync.Fori(1, groups) as g:
                for i in range(RING):
                    sp.wait_ge(lo_done, g * RING + (i + 1 - RING))
                    sp.dma_start(w_raw[:, i], weights[g * RING + i]).then_inc(raw_landed[i], 16)
            for c in range(groups * RING, N_CHUNKS):
                sp.wait_ge(lo_done, c + 1 - RING)
                sp.dma_start(w_raw[:, c % RING], weights[c]).then_inc(raw_landed[c % RING], 16)
            for t in range(TILES):
                sp.wait_ge(x_updated, 4 * 3 + t + 1)
                part = slice(0, SEQ if t == TILES - 1 else DIM)
                sp.dma_start(out_tiles[t][:, part], x[:, t, part]).then_inc(stored, 16)
            sp.wait_ge(stored, 16 * (TILES + 1))

        @block.gpsimd
        def _(pool):
            steps = [0]

            def low(c, group=0):
                pool.wait_ge(hi_done, group * RING + (c + 1))
                nc.gpsimd.tensor_tensor(w_lo[:, c % RING], w_raw[:, c % RING],
                                        w_hi[:, c % RING].bitcast(F32), ALU.subtract).then_inc(lo_done, 1)

            def lows(c0, c1):
                n = (c1 - c0) // RING
                if n > 1:
                    with nc.gpsimd.Fori(0, n) as g:
                        for i in range(RING):
                            low(c0 + i, g)
                    c0 += n * RING
                for c in range(c0, c1):
                    low(c)

            def own(ins):
                steps[0] += 1
                ins.then_inc(pool_step, 1)
                pool.wait_ge(pool_step, steps[0])

            def rstd(to, of, size, eps, done):
                own(nc.gpsimd.tensor_scalar(of, of, 1.0 / size, eps, ALU.mult, ALU.add))
                nc.gpsimd.tensor_tensor(to, of, minus_half[:, 0:of.shape[1]], ALU.pow).then_inc(done, 1)

            def post_rstds(b, t):
                q = 4 * (b - 1) + t
                if b:
                    pool.wait_ge(post_summed, q + 1)
                    rstd(rstd_post[:, q:q + 1], sum_post[:, q:q + 1], DIM, RMS_EPS, post_rstd)

            def pre_rstds(b, t):
                q = 4 * b + t
                if b < 4:
                    pool.wait_ge(pre_summed, q + 1)
                    rstd(rstd_pre[:, q:q + 1], sum_pre[:, q:q + 1], DIM, RMS_EPS, pre_rstd)

            def boundary(b):
                for t in range(2):
                    post_rstds(b, t)
                    pre_rstds(b, t)
                post_rstds(b, 2)
                if b < 4:
                    low(AFTER[b])
                    low(AFTER[b] + 1)
                pre_rstds(b, 2)
                post_rstds(b, 3)
                if b < 4:
                    low(AFTER[b] + 2)
                pre_rstds(b, 3)
                if b < 4:
                    low(AFTER[b] + 3)

            own(nc.gpsimd.memset(minus_half[:], -0.5))
            boundary(0)
            lows(RING, OUT0)
            pool.wait_ge(tables_landed, 16 * 4)
            for t in range(TILES):
                pool.wait_ge(gate_done, t + 1)
                nc.gpsimd.tensor_tensor(ret_gate[:, t, :], ret_gate[:, t, :], gn[:], ALU.mult).then_inc(gate_scaled, 1)
            for h in range(RET):
                pool.wait_ge(ret_summed, TILES * (h + 1))
                rstd(gn_rstd[:, 4 * h:4 * h + 4], gn_sum[:, 4 * h:4 * h + 4], HEAD, GN_EPS, ret_rstd)
                y = ret_y_rows[:, h, :].rearrange("p (t d) -> p t d", d=HEAD)
                pool.wait_ge(ret_normed, h + 1)
                nc.gpsimd.tensor_tensor(y, y, ret_gate[:, :, h * HEAD:(h + 1) * HEAD], ALU.mult).then_inc(ret_y, 1)
            at = OUT0
            for b in range(1, 4):
                if b == 3:
                    lows(at, GATE1)
                    parts = w_hi[:, GATE1 % RING, :].rearrange("p (k m) -> p k m", m=P)
                    raw = w_raw[:, GATE1 % RING, :].rearrange("p (k m) -> p k m", m=P)
                    pool.wait_ge(hi_done, GATE1 + 1)
                    nc.gpsimd.tensor_tensor(parts[:, :, 32:32 + FOX], raw[:, :, 0:FOX],
                                            parts[:, :, 0:FOX].bitcast(F32), ALU.subtract).then_inc(lo_done, 1)
                    at = GATE1 + 1
                lows(at, AFTER[b])
                boundary(b)
                at = AFTER[b] + RING
            lows(at, N_CHUNKS)
            pool.wait_ge(last_summed, 1)
            own(nc.gpsimd.tensor_scalar(last_sum[:, 0:1], last_sum[:, 0:1], 1.0, RMS_EPS, ALU.mult, ALU.add))
            for t in range(TILES - 1):
                post_rstds(4, t)
            pool.wait_ge(last_summed, 2)
            own(nc.gpsimd.tensor_tensor(last_sum[:, 0:1], last_sum[:, 0:1], last_sum[:, 1:2], ALU.add))
            nc.gpsimd.tensor_tensor(rstd_post[:, 15:16], last_sum[:, 0:1], minus_half[:, 0:1], ALU.pow).then_inc(post_rstd, 1)

        @block.scalar
        def _(act):
            steps = [0]

            def own(ins):
                steps[0] += 1
                ins.then_inc(act_step, 1)
                act.wait_ge(act_step, steps[0])

            def high(c, group=0):
                if c >= RING:
                    act.wait_ge(chunk_used, group * RING + (c + 1 - RING))
                act.wait_ge(raw_landed[c % RING], group * 16 + 16 * (c // RING + 1))
                nc.scalar.activation(w_hi[:, c % RING], w_raw[:, c % RING], ACT.Copy).then_inc(hi_done, 1)

            def highs(c0, c1):
                n = (c1 - c0) // RING
                if n > 1:
                    with nc.scalar.Fori(0, n) as g:
                        for i in range(RING):
                            high(c0 + i, g)
                    c0 += n * RING
                for c in range(c0, c1):
                    high(c)

            def sum_post_squares(b, t):
                q = 4 * (b - 1) + t
                if t < 3:
                    act.wait_ge(y_done, 3 * (b - 1) + t + 1)
                else:
                    act.wait_ge(chunk_used, AFTER[b])
                if b == 4:
                    act.wait_ge(post_summed, q)
                    act.wait_ge(last_summed, 1)
                else:
                    act.wait_ge(pre_summed, 4 * b + t)
                nc.scalar.activation(squares[:], ps[:, 2 * t:2 * t + 2, :], ACT.Square,
                                     accum_out=sum_post[:, q:q + 1]).then_inc(post_summed, 1)

            def sum_pre_squares(b, t):
                q = 4 * b + t
                if b:
                    act.wait_ge(x_updated, q - 3)
                else:
                    act.wait_ge(x_landed[t], 16)
                if b:
                    act.wait_ge(post_summed, q - 3)
                elif t:
                    act.wait_ge(pre_summed, q)
                nc.scalar.activation(squares[:], x[:, t], ACT.Square,
                                     accum_out=sum_pre[:, q:q + 1]).then_inc(pre_summed, 1)

            def turned_high(b, t):
                act.wait_ge(h_turned, 4 * b + t + 1)
                nc.scalar.activation(h_hi[:, :, cols(t)],
                                     ps[:, 2 * t:2 * t + 2, :].rearrange("p a (k s) -> p (a k) s", s=P),
                                     ACT.Copy).then_inc(h_hi_done, 1)

            def boundary(b):
                def sums(t, post, pre):
                    if post and b:
                        sum_post_squares(b, t)
                    if pre and b < 4:
                        sum_pre_squares(b, t)

                sums(0, True, True)
                sums(1, True, True)
                sums(2, True, False)
                if b == 0:
                    high(AFTER[b])
                if b < 4:
                    turned_high(b, 0)
                if 0 < b < 4:
                    high(AFTER[b])
                if b < 4:
                    if b:
                        high(AFTER[b] + 1)
                    turned_high(b, 1)
                    if b == 0:
                        high(AFTER[b] + 1)
                    high(AFTER[b] + 2)
                sums(2, False, True)
                if b < 4:
                    high(AFTER[b] + 3)
                sums(3, True, True)
                if b < 4:
                    turned_high(b, 2)
                    turned_high(b, 3)
                if 0 < b < 3:
                    act.wait_ge(normed, 4 * b + 4)
                    act.dma_start(gain_pre[:], norms[b + 1, 0].partition_broadcast(P)).then_inc(gain_pre_landed, 16)
                if 0 < b < 4:
                    act.wait_ge(x_updated, 4 * b)
                    act.dma_start(gain_post[:], norms[b, 1].partition_broadcast(P)).then_inc(gain_post_landed, 16)

            def head_high(hd):
                act.wait_ge(head_done, hd + 1)
                nc.scalar.activation(h_hi[:, hd % KT, :], ps[:, 5 + 2 * (hd % 2), :], ACT.Copy).then_inc(head_hi, 1)

            def attention(heads, unit0, head0, also={}):
                n_units = TILES * heads
                for n in range(n_units + 7):
                    if n < n_units:
                        u, i = unit0 + n, QUERY_ORDER[n % TILES]
                        act.wait_ge(logits, u + 1)
                        nc.scalar.activation(work[:, n % 4, 0:(i + 1) * P], work[:, n % 4, 0:(i + 1) * P],
                                             ACT.Exp, bias=minus_max[:, u:u + 1], scale=-1.0,
                                             accum_out=row_sum[:, u:u + 1]).then_inc(exped, 1)
                    m = n - 3
                    if 0 <= m < n_units:
                        h, i, u = m // TILES, QUERY_ORDER[m % TILES], unit0 + m
                        act.wait_ge(probs_turned, u + 1)
                        if h >= 2:
                            act.wait_ge(head_done, head0 + h - 1)
                        elif unit0 == 0:
                            act.wait_ge(ret_out, RET - 1 + h)
                        nc.scalar.activation(probs_t[:, h % 2, 0:i + 1, cols(i)],
                                             ps[:, 4 + 2 * (u % 2), 0:(i + 1) * P].rearrange("p (j q) -> p j q", q=P),
                                             ACT.Copy).then_inc(probs_t_ready, 1)
                    m = n - 6
                    if m >= 0 and m % TILES == 3:
                        head_high(head0 + m // TILES)
                    if n in also:
                        also[n]()

            def ffn(c0, tile0):
                def pair(p, gate_bank, group=0, step=0):
                    at = group * step
                    high(c0 + RING + 2 * p, group if step else 0)
                    high(c0 + RING + 2 * p + 1, group if step else 0)
                    act.wait_ge(chunk_used, group * RING * bool(step) + (c0 + 2 * p + 2))
                    if tile0 + p >= 2:
                        act.wait_ge(product_done, at + (tile0 + p - 1))
                    nc.scalar.activation(work[:, p % 2, :], ps[:, gate_bank, :], ACT.Silu).then_inc(silu_done, 1)
                    act.wait_ge(product_done, at + (tile0 + p + 1))
                    nc.scalar.activation(prod_hi[:, at + p, :] if step else prod_hi[:, p, :],
                                         work[:, 2 + p % 2, :], ACT.Copy).then_inc(product_hi, 1)

                pair(0, 0)
                pair(1, 2)
                with nc.scalar.Fori(0, (FT - 2) // 2) as g:
                    pair(2, 1, g, 2)
                    pair(3, 5, g, 2)

            act.dma_start(ident[:], ident_in).then_inc(ident_landed, 16)
            act.dma_start(gain_pre[:], norms[0, 0].partition_broadcast(P)).then_inc(gain_pre_landed, 16)

            boundary(0)
            act.dma_start(decay[:], decay_in).then_inc(tables_landed, 16)
            act.dma_start(gn[:], gn_gain.partition_broadcast(P)).then_inc(tables_landed, 16)
            act.dma_start(masks[:], mask_in).then_inc(tables_landed, 16)
            act.dma_start(forget_b[0:FOX, :], forget_bias).then_inc(tables_landed, 16)
            highs(QK0 + RING, QK0 + 3 * RING)
            act.wait_ge(rel_copied, 1)
            act.dma_start(bias_rows.ap(), bias_row[0:MOBA, :].unsqueeze(1).to_broadcast([MOBA, P, DIFFS])).then_inc(rel_stored, 16)
            highs(QK0 + 3 * RING, RV0 + RING)
            act.wait_ge(rel_stored, 16)
            act.dma_start(rel[:], bass.AP(bias_rows, P - 1, [[DIFFS - 1, P], [P * DIFFS, MOBA], [1, SEQ]])).then_inc(rel_landed, 16)
            highs(RV0 + RING, OUT0)
            act.wait_ge(chunk_used, MV0)
            for t in range(TILES):
                nc.scalar.activation(ret_gate[:, t, :], ps[:, t, :], ACT.Silu).then_inc(gate_done, 1)

            def squares_of(h):
                act.wait_ge(ret_centred, h + 1)
                for t in range(TILES):
                    n = TILES * h + t
                    if n:
                        act.wait_ge(ret_summed, n)
                    nc.scalar.activation(squares[:, 0:P], ret_y_rows[:, h, cols(t)], ACT.Square,
                                         accum_out=gn_sum[:, n:n + 1]).then_inc(ret_summed, 1)

            def copy_moba_v(t):
                if t < TILES - 1:
                    act.wait_ge(moba_v_done, t + 1)
                else:
                    act.wait_ge(chunk_used, OUT0)
                nc.scalar.activation(moba_v[:, t, :], ps[:, 5 + 2 * (t % 2), :], ACT.Copy).then_inc(moba_v_read, 1)

            copy_moba_v(0)
            squares_of(0)
            squares_of(1)
            copy_moba_v(1)
            squares_of(2)

            def last_squares():
                squares_of(3)
                copy_moba_v(3)

            def load_gains():
                act.wait_ge(head_done, RET)
                act.dma_start(gain_post[:], norms[0, 1].partition_broadcast(P)).then_inc(gain_post_landed, 16)
                act.dma_start(gain_pre[:], norms[1, 0].partition_broadcast(P)).then_inc(gain_pre_landed, 16)

            attention(MOBA, 0, RET, {
                1: lambda: copy_moba_v(2), 2: last_squares, 4: lambda: head_high(0),
                5: lambda: head_high(1), 7: lambda: head_high(2), 8: lambda: head_high(3),
                9: lambda: high(OUT0), 12: lambda: high(OUT0 + 1), 14: load_gains,
                16: lambda: high(OUT0 + 2), 17: lambda: high(OUT0 + 3)})
            highs(OUT0 + RING, FIN0)
            boundary(1)
            ffn(FIN0, 0)
            highs(FOUT0 + RING, QK1)
            boundary(2)
            act.dma_start(select[0:FOX, :], select_in).then_inc(select_landed, 16)
            highs(QK1 + RING, GATE1 + RING + 1)
            act.wait_ge(forget_logit, 1)
            own(nc.scalar.activation(gate_work[0:FOX, 3, :], gate_work[0:FOX, 2, :], ACT.Exp))
            nc.scalar.activation(gate_work[0:FOX, 2, :], gate_work[0:FOX, 3, :], ACT.Ln, bias=1.0).then_inc(forget_log, 1)
            highs(GATE1 + RING + 1, OUT1 + RING - 1)

            def copy_v(*tiles):
                for t in tiles:
                    if t < TILES - 1:
                        act.wait_ge(v_done, t + 1)
                    else:
                        act.wait_ge(chunk_used, OUT1)
                    nc.scalar.activation(fox_v[:, t, SEQ:2 * SEQ], ps[:, 4 + t, :], ACT.Copy).then_inc(fox_v_read, 1)

            attention(FOX, TILES * MOBA, KT, {2: lambda: copy_v(0, 2), 3: lambda: copy_v(1, 3), 4: lambda: high(OUT1 + RING - 1)})
            highs(OUT1 + RING, FIN1)
            boundary(3)
            ffn(FIN1, FT)
            highs(FOUT1 + RING, N_CHUNKS)

            def last_mean_square(half):
                act.wait_ge(chunk_used, N_CHUNKS if half else FOUT1 + FT // 2)
                if half:
                    act.wait_ge(post_summed, 15)
                else:
                    act.wait_ge(pre_summed, 16)
                nc.scalar.activation(squares[:, 0:SEQ], ps[:, 6 + half, :], ACT.Square, scale=DIM ** -0.5,
                                     accum_out=last_sum[:, half:half + 1]).then_inc(last_summed, 1)

            last_mean_square(0)
            for t in range(TILES - 1):
                sum_post_squares(4, t)
            last_mean_square(1)
            act.wait_ge(x_updated, 17)
            act.dma_start(out_tiles[TILES - 1][:, SEQ:DIM], x[:, TILES - 1, SEQ:DIM]).then_inc(stored, 16)

        @block.vector
        def _(vec):
            steps = [0]

            def own(ins):
                steps[0] += 1
                ins.then_inc(vec_step, 1)
                vec.wait_ge(vec_step, steps[0])

            def post(b, t):
                q = 4 * (b - 1) + t
                row = work[:, 2 * (t % 2):2 * (t % 2) + 2, :].rearrange("p a s -> p (a s)")
                vec.wait_ge(gain_post_landed, 16 * b)
                vec.wait_ge(post_rstd, q + 1)
                if t >= 2:
                    vec.wait_ge(x_updated, q - 1)
                    if b < 4:
                        vec.wait_ge(h_turned, 4 * b + t - 1)
                own(nc.vector.scalar_tensor_tensor(
                    out=row, in0=ps[:, 2 * t:2 * t + 2, :].rearrange("p a s -> p (a s)"),
                    scalar=rstd_post[:, q:q + 1], in1=gain_post[:], op0=ALU.mult, op1=ALU.mult))
                nc.vector.tensor_tensor(x[:, t], x[:, t], row, ALU.add).then_inc(x_updated, 1)

            def pre(b, t):
                q = 4 * b + t
                row = work[:, 2 * (t % 2):2 * (t % 2) + 2, :].rearrange("p a s -> p (a s)")
                vec.wait_ge(gain_pre_landed, 16 * (b + 1))
                vec.wait_ge(pre_rstd, q + 1)
                if b:
                    vec.wait_ge(x_updated, q - 3)
                elif t >= 2:
                    vec.wait_ge(h_turned, q - 1)
                nc.vector.scalar_tensor_tensor(
                    out=row, in0=x[:, t], scalar=rstd_pre[:, q:q + 1], in1=gain_pre[:],
                    op0=ALU.mult, op1=ALU.mult).then_inc(normed, 1)

            def turned_low(b, t):
                vec.wait_ge(h_hi_done, 4 * b + t + 1)
                nc.vector.tensor_tensor(
                    h_lo[:, :, cols(t)], ps[:, 2 * t:2 * t + 2, :].rearrange("p a (k s) -> p (a k) s", s=P),
                    h_hi[:, :, cols(t)].bitcast(F32), ALU.subtract).then_inc(h_ready, 1)

            def boundary(b):
                if b in (2, 4):
                    vec.wait_ge(product_ready, FT * b // 2)
                if b:
                    post(b, 0)
                if b < 4:
                    pre(b, 0)
                if b:
                    post(b, 1)
                if b < 4:
                    pre(b, 1)
                    turned_low(b, 0)
                if b:
                    post(b, 2)
                if b < 4:
                    turned_low(b, 1)
                if b == 0:
                    vec.wait_ge(rel_rows_done, 2)
                    nc.vector.tensor_copy(bias_row[0:MOBA, :].rearrange("h (a s) -> h a s", a=2),
                                          ps[0:MOBA, 6:8, 0:DIFFS // 2]).then_inc(rel_copied, 1)
                if b < 4:
                    pre(b, 2)
                if b:
                    post(b, 3)
                if b < 4:
                    pre(b, 3)
                    turned_low(b, 2)
                    turned_low(b, 3)

            def evacuate(to, bank, scale=None):
                if scale is None:
                    ins = nc.vector.tensor_copy(to, ps[:, bank, :])
                else:
                    ins = nc.vector.tensor_scalar(to, ps[:, bank, :], scale, None, ALU.mult)
                ins.then_inc(evacuated, 1)

            def head_low(hd):
                vec.wait_ge(head_hi, hd + 1)
                nc.vector.tensor_tensor(h_lo[:, hd % KT, :], ps[:, 5 + 2 * (hd % 2), :],
                                        h_hi[:, hd % KT, :].bitcast(F32), ALU.subtract).then_inc(head_ready, 1)

            def attention(heads, unit0, head0, table, also={}):
                n_units = TILES * heads
                for n in range(n_units + 8):
                    if n < n_units:
                        u, h, i = unit0 + n, n // TILES, QUERY_ORDER[n % TILES]
                        vec.wait_ge(scored, u + 1)
                        if n >= 4:
                            vec.wait_ge(probs_turned, u - 3)
                        nc.vector.tensor_tensor_reduce(
                            work[:, n % 4, 0:(i + 1) * P], ps[:, u % 4, 0:(i + 1) * P], table(h, i),
                            -1.0, float(np.finfo(np.float32).max), ALU.add, ALU.min,
                            minus_max[:, u:u + 1]).then_inc(logits, 1)
                    m = n - 1
                    if 0 <= m < n_units:
                        u, i = unit0 + m, QUERY_ORDER[m % TILES]
                        vec.wait_ge(exped, u + 1)
                        own(nc.vector.reciprocal(row_rec[:, u:u + 1], row_sum[:, u:u + 1]))
                        nc.vector.tensor_scalar(work[:, m % 4, 0:(i + 1) * P], work[:, m % 4, 0:(i + 1) * P],
                                                row_rec[:, u:u + 1], None, ALU.mult).then_inc(probs, 1)
                    m = n - 7
                    if m >= 0 and m % TILES == 3:
                        head_low(head0 + m // TILES)
                    if n in also:
                        also[n]()

            def ffn(c0, tile0):
                def pair(p, up_bank, group=0, step=0):
                    at = group * step
                    vec.wait_ge(silu_done, at + (tile0 + p + 1))
                    if tile0 + p >= 2:
                        vec.wait_ge(product_ready, at + (tile0 + p - 1))
                    nc.vector.tensor_tensor(work[:, 2 + p % 2, :], work[:, p % 2, :], ps[:, up_bank, :],
                                            ALU.mult).then_inc(product_done, 1)
                    vec.wait_ge(product_hi, at + (tile0 + p + 1))
                    tile = at + p if step else p
                    nc.vector.tensor_tensor(prod_lo[:, tile, :], work[:, 2 + p % 2, :],
                                            prod_hi[:, tile, :].bitcast(F32), ALU.subtract).then_inc(product_ready, 1)

                pair(0, 1)
                pair(1, 3)
                with nc.vector.Fori(0, (FT - 2) // 2) as g:
                    pair(2, 3, g, 2)
                    pair(3, 7, g, 2)

            boundary(0)
            vec.wait_ge(rotary_landed, 16)
            for i in range(2 * RET):
                vec.wait_ge(chunk_used, QK0 + i + 1)
                to, bank = ret_qk[:, i, :], ps[:, i % 4, :]
                nc.vector.tensor_tensor(to, bank, rotary[:, 0, :], ALU.mult).then_inc(turned_parts, 1)
                if i:
                    vec.wait_ge(evacuated, i)
                nc.vector.tensor_tensor(turned[0:64, :], ps[64:128, i % 4, :], rotary[64:128, 1, :],
                                        ALU.mult).then_inc(turned_parts, 1)
                nc.vector.tensor_tensor(turned[64:128, :], ps[0:64, i % 4, :], rotary[0:64, 1, :],
                                        ALU.mult).then_inc(turned_parts, 1)
                vec.wait_ge(turned_parts, 3 * (i + 1))
                nc.vector.tensor_tensor(to, to, turned[:], ALU.add).then_inc(evacuated, 1)
            for i in range(2 * MOBA):
                vec.wait_ge(chunk_used, QK0 + 2 * RET + i + 1)
                evacuate(moba_qk[:, i, :], i % 4, SCALE if i < MOBA else None)
            vec.wait_ge(chunk_used, RG0)
            for t in range(TILES):
                evacuate(ret_v[:, t, :], 4 + t)
            vec.wait_ge(tables_landed, 16 * 4)
            vec.wait_ge(rel_landed, 16)

            def decays(h):
                for j in range(TILES):
                    vec.wait_ge(ret_scored, 4 * h + j + 1)
                    if h >= 2:
                        vec.wait_ge(ret_out, h - 1)
                    nc.vector.tensor_tensor(probs_t[:, h % 2, j, 0:SEQ - j * P], ps[:, j, 0:SEQ - j * P],
                                            decay[:, h, 0:SEQ - j * P], ALU.mult).then_inc(ret_decayed, 1)

            def by_tile(row):
                return row.rearrange("p (t d) -> p t d", d=HEAD)

            def centre(h):
                bank, mean = by_tile(ps[:, 4 + 2 * (h % 2), :]), gn_mean[:, 4 * h:4 * h + 4]
                vec.wait_ge(ret_out, h + 1)
                own(nc.vector.tensor_reduce(mean, bank, AX_X, ALU.add))
                own(nc.vector.tensor_scalar(mean, mean, 1.0 / HEAD, None, ALU.mult))
                nc.vector.tensor_tensor(by_tile(ret_y_rows[:, h, :]), bank, mean.unsqueeze(2).to_broadcast([P, TILES, HEAD]),
                                        ALU.subtract).then_inc(ret_centred, 1)

            def norm(h):
                y = by_tile(ret_y_rows[:, h, :])
                vec.wait_ge(ret_rstd, h + 1)
                vec.wait_ge(ret_centred, h + 1)
                nc.vector.tensor_tensor(
                    y, y, gn_rstd[:, 4 * h:4 * h + 4].unsqueeze(2).to_broadcast([P, TILES, HEAD]),
                    ALU.mult).then_inc(ret_normed, 1)

            for h in range(RET):
                decays(h)
                if h:
                    centre(h - 1)
                if h >= 2:
                    norm(h - 2)
            attention(MOBA, 0, RET, lambda h, i: rel[:, h, (TILES - 1 - i) * P:SEQ],
                      {0: lambda: norm(2), 1: lambda: centre(3), 3: lambda: norm(3), 5: lambda: head_low(0),
                       6: lambda: head_low(1), 8: lambda: head_low(2), 9: lambda: head_low(3)})
            boundary(1)
            ffn(FIN0, 0)
            boundary(2)
            first = 2 * (RET + MOBA) + TILES
            for scale, g0 in ((SCALE, 0), (None, FOX // 4)):
                with nc.vector.Fori(g0, g0 + FOX // 4) as g:
                    for i in range(4):
                        vec.wait_ge(chunk_used, g * 4 + (QK1 + i + 1))
                        evacuate(fox_qk[:, g * 4 + i, :], i, scale)
            vec.wait_ge(select_landed, 16)
            nc.vector.tensor_copy(select_r[0:FOX, :], select[0:FOX, :]).then_inc(select_ready, 1)
            z, low, neg, one, total = (gate_work[0:FOX, n, :] for n in range(5))
            vec.wait_ge(chunk_used, GATE1 + 1)
            own(nc.vector.tensor_scalar(z, ps[0:FOX, 4, :], forget_b[0:FOX, :], None, ALU.add))
            own(nc.vector.tensor_copy(low, ps[32:32 + FOX, 4, :]))
            own(nc.vector.tensor_tensor(z, z, low, ALU.add))
            own(nc.vector.tensor_scalar(low, z, 0.0, None, ALU.min))
            nc.vector.scalar_tensor_tensor(out=neg, in0=low, scalar=2.0, in1=z, op0=ALU.mult,
                                           op1=ALU.subtract).then_inc(forget_logit, 1)
            vec.wait_ge(forget_log, 1)
            own(nc.vector.tensor_tensor(z, low, neg, ALU.subtract))
            own(nc.vector.memset(one, 1.0))
            own(nc.vector.tensor_tensor_scan(total, one, z, 0.0, ALU.mult, ALU.add))
            own(nc.vector.tensor_copy(f_hi[0:FOX, :], total))
            nc.vector.tensor_tensor(f_lo[0:FOX, :], total, f_hi[0:FOX, :].bitcast(F32), ALU.subtract).then_inc(f_ready, 1)
            vec.wait_ge(chunk_used, V1 + 4)
            for t in range(TILES):
                evacuate(fox_v[:, t, 0:SEQ], t)
            for h in range(FOX):
                vec.wait_ge(f_spread, h + 1)
                evacuate(minus_f[:, h, :], h % TILES)
            attention(FOX, TILES * MOBA, KT, lambda h, i: minus_f[:, h, 0:(i + 1) * P])
            boundary(3)
            ffn(FIN1, FT)
            vec.wait_ge(product_ready, 2 * FT)
            for t in range(TILES - 1):
                post(4, t)
            vec.wait_ge(x_updated, 14)
            for half in range(2):
                at = slice(half * SEQ, (half + 1) * SEQ)
                vec.wait_ge(last_summed, half + 1)
                own(nc.vector.tensor_tensor(work[:, 2 + half, :], ps[:, 6 + half, :], gain_post[:, at], ALU.mult))
            vec.wait_ge(post_rstd, 16)
            for half in range(2):
                at = slice(half * SEQ, (half + 1) * SEQ)
                nc.vector.scalar_tensor_tensor(
                    out=x[:, TILES - 1, at], in0=work[:, 2 + half, :], scalar=rstd_post[:, 15:16],
                    in1=x[:, TILES - 1, at], op0=ALU.mult, op1=ALU.add).then_inc(x_updated, 1)

        @block.tensor
        def _(pe):
            mm = nc.tensor.matmul

            def exact(to, held, moved, start, stop):
                mm(to, held[0], moved[0], start=start, stop=False)
                mm(to, held[0], moved[1], start=False, stop=False)
                return mm(to, held[1], moved[0], start=False, stop=stop)

            def column_chunk(c, bank, at=slice(0, SEQ)):
                for k in range(KT):
                    last = exact(ps[:, bank, at], [w[:, c % RING, cols(k)] for w in (w_hi, w_lo)],
                                 [h[:, k, at] for h in (h_hi, h_lo)], k == 0, k == KT - 1)
                return last

            def row_chunk(c, k0, n_k, banks, tiles=range(TILES), source=(h_hi, h_lo), done=None):
                for kk in range(2):
                    k = k0 + kk
                    for t in tiles:
                        last = exact(ps[:, banks[t], :], [s[:, k, cols(t)] for s in source],
                                     [w[:, c % RING, kk * SEQ:(kk + 1) * SEQ] for w in (w_hi, w_lo)],
                                     k == 0, k == n_k - 1)
                        if done is not None and k == n_k - 1 and t < TILES - 1:
                            last.then_inc(done, 1)
                return last

            def turn(b, t):
                pe.wait_ge(normed, 4 * b + t + 1)
                if (b, t) == (0, TILES - 1):
                    pe.wait_ge(rel_copied, 1)
                for k in range(KT):
                    last = nc.tensor.transpose(ps[:, 2 * t + k // 4, cols(k % 4)],
                                               work[:, 2 * (t % 2) + k // 4, cols(k % 4)], ident[:])
                last.then_inc(h_turned, 1)

            def first_columns(b):
                c0 = AFTER[b]
                pe.wait_ge(h_ready, 4 * b + 2)
                for i in range(RING):
                    if i == RING - 1:
                        turn(b, 2)
                        turn(b, 3)
                    pe.wait_ge(lo_done, c0 + i + 1)
                    column_chunk(c0 + i, i, slice(0, SEQ // 2))
                pe.wait_ge(h_ready, 4 * b + 4)
                for i in range(RING):
                    column_chunk(c0 + i, i, slice(SEQ // 2, SEQ)).then_inc(chunk_used, 1)

            def rows(c0, n, n_k, banks, source=(h_hi, h_lo), ready=None, k0=0):
                for i in range(n):
                    if ready is not None:
                        ready(k0 + 2 * i + 1)
                    pe.wait_ge(lo_done, c0 + i + 1)
                    row_chunk(c0 + i, k0 + 2 * i, n_k, banks, source=source).then_inc(chunk_used, 1)

            def last_rows(b, k0, n_k, banks, source=(h_hi, h_lo)):
                c0 = AFTER[b] - RING
                for t in range(TILES):
                    for i in range(RING):
                        if t == 0:
                            pe.wait_ge(lo_done, c0 + i + 1)
                        if b < 4 and t == TILES - 1 and i in (0, 2):
                            turn(b, i // 2)
                        last = row_chunk(c0 + i, k0 + 2 * i, n_k, banks, (t,), source)
                        if t == TILES - 1:
                            last.then_inc(chunk_used, 1)
                        elif i == RING - 1:
                            last.then_inc(y_done, 1)

            halves = [[2 * t + half for t in range(TILES)] for half in range(2)]

            def filler(heads, unit0, c0):
                def tile(t):
                    if t == 0:
                        pe.wait_ge(logits, unit0 + TILES * heads)
                        pe.wait_ge(lo_done, c0 + 1)
                    row_chunk(c0, 0, KT, halves[0], (t,))
                last = TILES * heads
                return {last + 1: lambda: tile(0), last + 2: lambda: tile(1)}

            def project_out(b, c0, head0):
                def ready(k):
                    pe.wait_ge(head_ready, head0 + k + 1)
                row_chunk(c0, 0, KT, halves[0], (2, 3)).then_inc(chunk_used, 1)
                rows(c0 + 1, 3, KT, halves[0], ready=ready, k0=2)
                last_rows(b, 0, KT, halves[1])

            def ffn(b, c_in, c_out, tile0):
                first_columns(b)
                with nc.tensor.Fori(0, (2 * FT - RING) // RING) as g:
                    for i in range(RING):
                        p = (RING + i) // 2
                        pe.wait_ge(product_done, g * 2 + (tile0 + p - 1 + i % 2))
                        pe.wait_ge(lo_done, g * RING + (c_in + RING + i + 1))
                        column_chunk((c_in + i) % RING, 2 * i + 1).then_inc(chunk_used, 1)

                def ready(k):
                    pe.wait_ge(product_ready, tile0 + k + 1)
                source = (prod_hi, prod_lo)
                rows(c_out, FT // 2, FT, halves[0], source, ready)
                rows(c_out + FT // 2, FT // 2 - RING, FT, halves[1], source)
                last_rows(b + 1, FT - 2 * RING, FT, halves[1], source)

            def attention(heads, unit0, head0, q, k, v, masked, also={}, part=None):
                n_units = TILES * heads
                for n in range(n_units + 6 if part != 0 else TILES):
                    if n < n_units and (n >= TILES or part != 1):
                        u, h, i = unit0 + n, n // TILES, QUERY_ORDER[n % TILES]
                        if n >= 4:
                            pe.wait_ge(logits, u - 3)
                        elif masked:
                            pe.wait_ge(evacuated, first + 2 * FOX + TILES + TILES + n + 1)
                        else:
                            pe.wait_ge(ret_decayed, 4 * (RET - 1) + n + 1)
                        last = mm(ps[:, u % 4, 0:(i + 1) * P], q[:, h, cols(i)], k[:, h, 0:(i + 1) * P],
                                  start=True, stop=True)
                        if masked:
                            last = mm(ps[:, u % 4, cols(i)], masks[:, 0:P], masks[:, P:2 * P],
                                      start=False, stop=True, skip_group_check=True)
                        last.then_inc(scored, 1)
                    if part == 0:
                        continue
                    m = n - 3
                    if 0 <= m < n_units:
                        u, i = unit0 + m, QUERY_ORDER[m % TILES]
                        pe.wait_ge(probs, u + 1)
                        if u >= 2:
                            pe.wait_ge(probs_t_ready, u - 1)
                            if masked and m < 2:
                                pe.wait_ge(fox_v_read, m + 1)
                        else:
                            pe.wait_ge(ret_centred, RET - 1 + u)
                        for j in range(i + 1):
                            last = nc.tensor.transpose(ps[:, 4 + 2 * (u % 2), cols(j)],
                                                       work[:, m % 4, cols(j)], ident[:])
                        last.then_inc(probs_turned, 1)
                    m = n - 5
                    if m >= 0 and m % TILES == 3:
                        h, hd = m // TILES, head0 + m // TILES
                        pe.wait_ge(probs_t_ready, unit0 + m + 1)
                        if hd >= 2:
                            pe.wait_ge(head_ready, hd - 1)
                        if hd == KT:
                            pe.wait_ge(fox_v_read, TILES)
                        for j in range(TILES):
                            last = mm(ps[:, 5 + 2 * (hd % 2), j * P:SEQ], v[:, j, h * HEAD:(h + 1) * HEAD],
                                      probs_t[:, h % 2, j, j * P:SEQ], start=j == 0, stop=j == TILES - 1)
                        last.then_inc(head_done, 1)
                    if n in also:
                        also[n]()

            pe.wait_ge(ident_landed, 16)
            def warm(n):
                for _ in range(n):
                    mm(ps[:, 7, 0:P], ident[:], ident[:], start=True, stop=True)
            warm(9)
            turn(0, 0)
            turn(0, 1)
            warm(4)
            pe.wait_ge(rel_in_landed, 32)
            for half in range(2):
                mm(ps[0:MOBA, 6 + half, 0:DIFFS // 2], rel_table[0:BUCKETS + 1, :],
                   onehot[0:BUCKETS + 1, half * (DIFFS // 2):(half + 1) * (DIFFS // 2)],
                   start=True, stop=True).then_inc(rel_rows_done, 1)
            first_columns(0)
            with nc.tensor.Fori(1, (RV0 - QK0) // RING) as g:
                for i in range(RING):
                    pe.wait_ge(evacuated, g * RING + (i + 1 - RING))
                    pe.wait_ge(lo_done, g * RING + (QK0 + i + 1))
                    column_chunk(i, i).then_inc(chunk_used, 1)
            rows(RV0, 4, KT, [4, 5, 6, 7])
            pe.wait_ge(evacuated, RV0)
            rows(RG0, 4, KT, [0, 1, 2, 3])
            pe.wait_ge(evacuated, RV0 + TILES)

            def moba_values(t):
                if t >= 2:
                    pe.wait_ge(moba_v_read, t - 1)
                for i in range(RING):
                    if t == 0:
                        pe.wait_ge(lo_done, MV0 + i + 1)
                    last = row_chunk(MV0 + i, 2 * i, KT, [5 + 2 * (t % 2)] * TILES, (t,))
                    if t == TILES - 1:
                        last.then_inc(chunk_used, 1)
                    elif i == RING - 1:
                        last.then_inc(moba_v_done, 1)


            def ret_scores(h):
                for j in range(TILES):
                    if h >= 1:
                        pe.wait_ge(ret_decayed, 4 * (h - 1) + j + 1)
                    else:
                        pe.wait_ge(gate_done, j + 1)
                    mm(ps[:, j, 0:SEQ - j * P], ret_qk[:, RET + h, cols(j)], ret_qk[:, h, j * P:SEQ],
                       start=True, stop=True).then_inc(ret_scored, 1)

            def ret_output(h):
                pe.wait_ge(ret_decayed, 4 * h + 4)
                if h >= 2:
                    pe.wait_ge(ret_centred, h - 1)
                for i in range(TILES):
                    for j in range(i + 1):
                        last = mm(ps[:, 4 + 2 * (h % 2), cols(i)], probs_t[:, h % 2, j, cols(i - j)],
                                  ret_v[:, j, h * HEAD:(h + 1) * HEAD], start=j == 0, stop=j == i)
                last.then_inc(ret_out, 1)

            def ret_turn(h):
                pe.wait_ge(ret_y, h + 1)
                if h >= 2:
                    pe.wait_ge(head_ready, h - 1)
                else:
                    pe.wait_ge(moba_v_read, h + 3)
                for t in range(TILES):
                    last = nc.tensor.transpose(ps[:, 5 + 2 * (h % 2), cols(t)], ret_y_rows[:, h, cols(t)], ident[:])
                last.then_inc(head_done, 1)

            moba_values(0)
            ret_scores(0)
            ret_scores(1)
            ret_output(0)
            ret_scores(2)
            ret_output(1)
            moba_values(1)
            ret_scores(3)
            ret_output(2)

            def last_output():
                moba_values(2)
                ret_output(3)

            attention(MOBA, 0, RET, moba_qk[:, 0:MOBA], moba_qk[:, MOBA:2 * MOBA], moba_v, False,
                      {1: last_output, 2: lambda: moba_values(3), 3: lambda: ret_turn(0),
                       4: lambda: ret_turn(1), 6: lambda: ret_turn(2), 7: lambda: ret_turn(3),
                       **filler(MOBA, 0, OUT0)})
            project_out(1, OUT0, 0)
            ffn(1, FIN0, FOUT0, 0)
            first = 2 * (RET + MOBA) + TILES
            first_columns(2)
            with nc.tensor.Fori(1, 2 * FOX // RING) as g:
                for i in range(RING):
                    pe.wait_ge(evacuated, g * RING + (first + i + 1 - RING))
                    pe.wait_ge(lo_done, g * RING + (QK1 + i + 1))
                    column_chunk((QK1 + i) % RING, i).then_inc(chunk_used, 1)
            pe.wait_ge(lo_done, GATE1 + 1)
            for k in range(KT):
                mm(ps[:, 4, :], w_hi[:, GATE1 % RING, cols(k)], h_hi[:, k, :], start=k == 0, stop=False)
                last = mm(ps[:, 4, :], w_hi[:, GATE1 % RING, cols(k)], h_lo[:, k, :], start=False, stop=k == KT - 1)
            last.then_inc(chunk_used, 1)
            pe.wait_ge(evacuated, first + 2 * FOX)
            rows(V1, 4, KT, [0, 1, 2, 3])
            pe.wait_ge(f_ready, 1)
            pe.wait_ge(select_ready, 1)

            def spread(h):
                pe.wait_ge(evacuated, first + 2 * FOX + h + 1)
                mm(ps[:, h % TILES, :], select_r[0:FOX, cols(h)], f_hi[0:FOX, :], start=True, stop=False)
                mm(ps[:, h % TILES, :], select_r[0:FOX, cols(h)], f_lo[0:FOX, :],
                   start=False, stop=True).then_inc(f_spread, 1)

            def fox(part):
                attention(FOX, TILES * MOBA, KT, fox_qk[:, 0:FOX], fox_qk[:, FOX:2 * FOX], fox_v, True,
                          filler(FOX, TILES * MOBA, OUT1), part)

            for i in range(3):
                rows(V1 + 4 + i, 1, KT, [4, 5, 6, 7], k0=2 * i)
                for h in ((0, 1), (2, 3), (4, 5, 6, 7))[i]:
                    spread(h)
            fox(0)
            pe.wait_ge(lo_done, V1 + 8)
            row_chunk(V1 + 7, 6, KT, [4, 5, 6, 7], done=v_done).then_inc(chunk_used, 1)
            fox(1)
            project_out(3, OUT1, KT)
            ffn(3, FIN1, FOUT1, FT)


def constants():
    f32 = np.float32
    ident = np.eye(P, dtype=f32)
    mask = np.where(np.arange(P)[None, :] > np.arange(P)[:, None], NEG, 0.0)
    gap = np.arange(SEQ)[None, :] - np.arange(P)[:, None]
    log_g = np.log1p(-(2.0 ** (-5.0 - np.arange(RET))))
    decay = np.where(gap[:, None, :] >= 0, np.exp(log_g[None, :, None] * np.maximum(gap, 0)[:, None, :]), 0.0)
    inv = np.power(f32(10000.0), -np.arange(0, HEAD, 2, dtype=f32) / f32(HEAD)).astype(f32)
    angle = (np.arange(SEQ, dtype=f32)[None, :] * inv[:, None]).astype(f32).astype(np.float64)
    cos, sin = np.cos(angle), np.sin(angle)
    rotary = np.stack([np.concatenate([cos, cos]), np.concatenate([sin, -sin])], axis=1)
    rel = SEQ - 1 - np.arange(DIFFS)
    n = np.maximum(rel, 0)
    exact = BUCKETS // 2
    large = exact + (np.log(np.maximum(n, 1).astype(f32) / exact) / np.log(128 / exact)
                     * (BUCKETS - exact)).astype(np.int32)
    bucket = np.where(n < exact, n, np.minimum(large, BUCKETS - 1))
    onehot = np.zeros((BUCKETS + 1, DIFFS), f32)
    onehot[bucket, np.arange(DIFFS)] = rel >= 0
    onehot[BUCKETS] = np.where(rel < 0, NEG, 0.0)
    select = -np.repeat(np.eye(FOX, dtype=f32), P, axis=1)
    return ident, mask, (decay * SCALE).astype(f32), rotary.astype(f32), onehot, select


def column_chunks(w):
    n = w.shape[1] // P
    return w.reshape(KT, P, n, P).transpose(2, 1, 0, 3).reshape(n, P, KT * P)


def row_chunks(w):
    k, n = w.shape[0] // (2 * P), w.shape[1] // SEQ
    return w.reshape(k, 2, P, n, SEQ).transpose(3, 0, 2, 1, 4).reshape(n * k, P, 2 * SEQ)


def ffn_chunks(w_in, w_out):
    both = np.stack([column_chunks(w_in[:, :HIDDEN]), column_chunks(w_in[:, HIDDEN:])], axis=1)
    return [both.reshape(2 * FT, P, CHUNK), row_chunks(w_out)]


def kernel(x, rel_bias, norm_mix_pre, norm_mix_post, norm_ffn_pre, norm_ffn_post, even_w_in, even_gn,
           even_w_out, odd_w_in, odd_b_forget, odd_w_out, ffn_w_in, ffn_w_out):
    import concourse.bacc as bacc
    from concourse.bass_utils import run_bass_kernel_spmd
    import ml_dtypes

    a = np.asarray
    even, odd = a(even_w_in)[0], a(odd_w_in)[0]
    ffn_in, ffn_out = a(ffn_w_in), a(ffn_w_out)
    rw, mw, fw = RET * HEAD, MOBA * HEAD, FOX * HEAD
    q_and_k = np.concatenate([even[:, :2 * rw], even[:, 4 * rw:4 * rw + 2 * mw]], axis=1)
    gate = np.concatenate([odd[:, 3 * fw:], np.zeros((DIM, P - FOX), np.float32)], axis=1)
    stream = np.concatenate([
        column_chunks(q_and_k), row_chunks(even[:, 2 * rw:3 * rw]), row_chunks(even[:, 3 * rw:4 * rw]),
        row_chunks(even[:, 4 * rw + 2 * mw:]), row_chunks(a(even_w_out)[0]),
        *ffn_chunks(ffn_in[0], ffn_out[0]),
        column_chunks(odd[:, :2 * fw]), column_chunks(gate), row_chunks(odd[:, 2 * fw:3 * fw]),
        row_chunks(a(odd_w_out)[0]),
        *ffn_chunks(ffn_in[1], ffn_out[1]),
    ])
    assert stream.shape == (N_CHUNKS, P, CHUNK)
    pre = [a(norm_mix_pre)[0], a(norm_ffn_pre)[0], a(norm_mix_pre)[1], a(norm_ffn_pre)[1]]
    post = [a(norm_mix_post)[0], a(norm_ffn_post)[0], a(norm_mix_post)[1], a(norm_ffn_post)[1]]
    ident, mask, decay, rotary, onehot, select = constants()
    arrays = {
        "x_in": a(x)[0],
        "weights": stream,
        "norms": np.stack([np.stack(pre), np.stack(post)], axis=1),
        "gn_gain": a(even_gn)[0],
        "rel_bias": np.concatenate([a(rel_bias), np.ones((1, MOBA), np.float32)]),
        "forget_bias": a(odd_b_forget)[0][:, None],
        "ident_in": ident,
        "mask_in": np.concatenate([ident, mask], axis=1).astype(ml_dtypes.bfloat16),
        "decay_in": decay,
        "rotary_in": rotary,
        "onehot_in": onehot,
        "select_in": select,
    }
    nc = bacc.Bacc("TRN2", target_bir_lowering=False, num_devices=1)
    arrays = {n: np.ascontiguousarray(v) for n, v in arrays.items()}
    args = {n: nc.dram_tensor(n, v.shape, mybir.dt.from_np(v.dtype), kind="ExternalInput").ap()
            for n, v in arrays.items()}
    out = nc.dram_tensor("out", (SEQ, DIM), F32, kind="ExternalOutput").ap()
    build(nc, **args, out=out)
    result = run_bass_kernel_spmd(nc, [arrays], core_ids=[0])
    return result.results[0]["out"].reshape(1, SEQ, DIM)
```
